# Optimizing a Trainium2 kernel written in Bass

```python
import math
import jax, jax.numpy as jnp
from jax import lax
import numpy as np

D_MODEL = 1024
BATCH = 1
SEQ = 1024
DEPTH = 1

N_HEADS = 8
HEAD_DIM = 64
V_HEAD_DIM = 2 * HEAD_DIM
ATTN_QK_WIDTH = 2 * N_HEADS * HEAD_DIM
ATTN_V_WIDTH = N_HEADS * V_HEAD_DIM
Q_BLOCK = 128
POOL_WINDOWS = (2, 4, 8, 16)
POOL_GROUPS = len(POOL_WINDOWS)
POOL_GROUP_DIM = 128
POOL_WIDTH = POOL_GROUPS * POOL_GROUP_DIM
N_BRANCHES = 2
IN_WIDTH = 2 * ATTN_QK_WIDTH + ATTN_V_WIDTH + POOL_WIDTH + N_BRANCHES * D_MODEL
PEER_HEADS = 8
PEER_KEYS = 128
PEER_EXPERTS = PEER_KEYS * PEER_KEYS
PEER_QUERY_DIM = 256
PEER_HALF = PEER_QUERY_DIM // 2
PEER_TOPK = 16
PEER_CHUNK = 128
DN_ALPHA = (2.0 * DEPTH) ** 0.25
DN_BETA = (8.0 * DEPTH) ** -0.25
LN_EPS = 1e-5

kernel_name = "hybrid_diffattn_pool_peer_deepnorm"

def layer_norm(x, g, b):
    xf = x.astype(jnp.float32)
    mu = jnp.mean(xf, axis=-1, keepdims=True)
    var = jnp.mean(jnp.square(xf - mu), axis=-1, keepdims=True)
    return ((xf - mu) * lax.rsqrt(var + LN_EPS) * g.astype(jnp.float32) + b.astype(jnp.float32)).astype(x.dtype)

def rms_norm(x, g):
    xf = x.astype(jnp.float32)
    return (xf * lax.rsqrt(jnp.mean(xf * xf, axis=-1, keepdims=True) + LN_EPS) * g.astype(jnp.float32)).astype(x.dtype)

def alibi_slopes(n):
    return jnp.asarray(np.array([2.0 ** (-8.0 * (h + 1) / n) for h in range(n)], dtype=np.float32))

def diff_attention(q1, q2, k1, k2, v, lam, slopes):
    S = q1.shape[2]
    scale = HEAD_DIM ** -0.5
    outs = []
    for blk in range(S // Q_BLOCK):
        lo, hi = blk * Q_BLOCK, (blk + 1) * Q_BLOCK
        dist = (jnp.arange(lo, hi)[:, None] - jnp.arange(hi)[None, :]).astype(jnp.float32)
        bias = jnp.where(dist[None] >= 0, -slopes[:, None, None] * dist[None], -jnp.inf)

        def probs(q, k):
            s = jnp.einsum('bhqd,bhkd->bhqk', q[:, :, lo:hi], k[:, :, :hi]).astype(jnp.float32) * scale
            return jax.nn.softmax(s + bias[None], axis=-1)

        a = probs(q1, k1) - lam * probs(q2, k2)
        outs.append(jnp.einsum('bhqk,bhkd->bhqd', a.astype(v.dtype), v[:, :, :hi]))
    return jnp.concatenate(outs, axis=2)

def multiscale_pool(p):
    S = p.shape[1]
    pf = p.astype(jnp.float32)
    cs = jnp.cumsum(pf, axis=1)
    wmax = max(POOL_WINDOWS)
    cs_pad = jnp.pad(cs, ((0, 0), (wmax, 0), (0, 0)))
    t = jnp.arange(S, dtype=jnp.float32)[None, :, None]
    groups = []
    for gi, w in enumerate(POOL_WINDOWS):
        sl = slice(gi * POOL_GROUP_DIM, (gi + 1) * POOL_GROUP_DIM)
        lagged = cs_pad[:, wmax - w: wmax - w + S, sl]
        cnt = jnp.minimum(float(w), t + 1.0)
        groups.append((cs[:, :, sl] - lagged) / cnt - pf[:, :, sl])
    return jnp.stack(groups, axis=2)

def hybrid_mixer(x, w_in, b_gate, lq1, lk1, lq2, lk2, subln_g, w_attn_proj,
                 pool_w, pool_scale, w_pool_proj, w_out, lam_init):
    B, S, _ = x.shape
    h = x @ w_in
    q, k, v, p, g = jnp.split(h, [ATTN_QK_WIDTH, 2 * ATTN_QK_WIDTH, 2 * ATTN_QK_WIDTH + ATTN_V_WIDTH,
                                  2 * ATTN_QK_WIDTH + ATTN_V_WIDTH + POOL_WIDTH], axis=-1)
    q = q.reshape(B, S, N_HEADS, 2, HEAD_DIM).transpose(3, 0, 2, 1, 4)
    k = k.reshape(B, S, N_HEADS, 2, HEAD_DIM).transpose(3, 0, 2, 1, 4)
    v = v.reshape(B, S, N_HEADS, V_HEAD_DIM).transpose(0, 2, 1, 3)
    f32 = jnp.float32
    lam = (jnp.exp(jnp.sum(lq1.astype(f32) * lk1.astype(f32)))
           - jnp.exp(jnp.sum(lq2.astype(f32) * lk2.astype(f32))) + lam_init)
    o = diff_attention(q[0], q[1], k[0], k[1], v, lam, alibi_slopes(N_HEADS))
    o = rms_norm(o, subln_g) * (1.0 - lam_init)
    o = o.transpose(0, 2, 1, 3).reshape(B, S, ATTN_V_WIDTH)
    attn_branch = o @ w_attn_proj
    pooled = multiscale_pool(p).astype(x.dtype)
    pm = jnp.einsum('bsgc,gcd->bsgd', pooled, pool_w).reshape(B, S, POOL_WIDTH) * pool_scale
    pool_branch = pm @ w_pool_proj
    gates = jax.nn.sigmoid((g + b_gate).astype(f32)).astype(x.dtype)
    g_attn, g_pool = jnp.split(gates, N_BRANCHES, axis=-1)
    merged = g_attn * attn_branch + g_pool * pool_branch
    return merged @ w_out

def peer_ffn(y, w_q, sub_keys, u, v):
    B, S, D = y.shape
    T = B * S
    yc = y.reshape(T // PEER_CHUNK, PEER_CHUNK, D)

    def chunk(yb):
        q = (yb @ w_q).reshape(PEER_CHUNK, PEER_HEADS, 2, PEER_HALF)
        s = jnp.einsum('chpk,hpnk->chpn', q, sub_keys).astype(jnp.float32)
        s1, i1 = lax.top_k(s[:, :, 0], PEER_TOPK)
        s2, i2 = lax.top_k(s[:, :, 1], PEER_TOPK)
        cand = (s1[..., :, None] + s2[..., None, :]).reshape(PEER_CHUNK, PEER_HEADS, PEER_TOPK * PEER_TOPK)
        sc, ci = lax.top_k(cand, PEER_TOPK)
        row = jnp.take_along_axis(i1, ci // PEER_TOPK, axis=-1)
        col = jnp.take_along_axis(i2, ci % PEER_TOPK, axis=-1)
        idx = row * PEER_KEYS + col
        gate = jax.nn.softmax(sc, axis=-1)
        act = jax.nn.gelu(jnp.einsum('ched,cd->che', u[idx], yb), approximate=False)
        return jnp.einsum('che,ched->cd', (gate * act).astype(yb.dtype), v[idx])

    return lax.map(chunk, yc).reshape(B, S, D)

def setup_inputs(seed: int = 0) -> dict:
    key = jax.random.key(seed)
    ks = jax.random.split(key, 22)
    n = lambda k, shape, s: jax.random.normal(k, shape, jnp.float32) * s
    L, D = DEPTH, D_MODEL
    return {
        "x": n(ks[0], (BATCH, SEQ, D), 1.0),
        "w_in": n(ks[1], (L, D, IN_WIDTH), D ** -0.5),
        "b_gate": n(ks[2], (L, N_BRANCHES * D), 0.01),
        "lambda_q1": n(ks[3], (L, HEAD_DIM), 0.1),
        "lambda_k1": n(ks[4], (L, HEAD_DIM), 0.1),
        "lambda_q2": n(ks[5], (L, HEAD_DIM), 0.1),
        "lambda_k2": n(ks[6], (L, HEAD_DIM), 0.1),
        "subln_g": 1.0 + n(ks[7], (L, V_HEAD_DIM), 0.02),
        "w_attn_proj": n(ks[8], (L, ATTN_V_WIDTH, D), ATTN_V_WIDTH ** -0.5 * DN_BETA),
        "pool_w": n(ks[9], (L, POOL_GROUPS, POOL_GROUP_DIM, POOL_GROUP_DIM), POOL_GROUP_DIM ** -0.5),
        "pool_scale": 1.0 + n(ks[10], (L, POOL_WIDTH), 0.02),
        "w_pool_proj": n(ks[11], (L, POOL_WIDTH, D), POOL_WIDTH ** -0.5 * DN_BETA),
        "w_out": n(ks[12], (L, D, D), D ** -0.5 * DN_BETA),
        "ln1_g": 1.0 + n(ks[13], (L, D), 0.02),
        "ln1_b": n(ks[14], (L, D), 0.01),
        "peer_wq": n(ks[15], (L, D, PEER_HEADS * PEER_QUERY_DIM), D ** -0.5),
        "peer_subkeys": n(ks[16], (L, PEER_HEADS, 2, PEER_KEYS, PEER_HALF), PEER_HALF ** -0.5),
        "peer_u": n(ks[17], (L, PEER_EXPERTS, D), D ** -0.5),
        "peer_v": n(ks[18], (L, PEER_EXPERTS, D), DN_BETA),
        "ln2_g": 1.0 + n(ks[19], (L, D), 0.02),
        "ln2_b": n(ks[20], (L, D), 0.01),
    }

def reference(x, w_in, b_gate, lambda_q1, lambda_k1, lambda_q2, lambda_k2, subln_g, w_attn_proj,
              pool_w, pool_scale, w_pool_proj, w_out, ln1_g, ln1_b, peer_wq, peer_subkeys,
              peer_u, peer_v, ln2_g, ln2_b):
    h = x
    for l in range(DEPTH):
        lam_init = 0.8 - 0.6 * math.exp(-0.3 * l)
        mix = hybrid_mixer(h, w_in[l], b_gate[l], lambda_q1[l], lambda_k1[l], lambda_q2[l], lambda_k2[l],
                           subln_g[l], w_attn_proj[l], pool_w[l], pool_scale[l], w_pool_proj[l],
                           w_out[l], lam_init)
        h = layer_norm(DN_ALPHA * h + mix, ln1_g[l], ln1_b[l])
        ffn = peer_ffn(h, peer_wq[l], peer_subkeys[l], peer_u[l], peer_v[l])
        h = layer_norm(DN_ALPHA * h + ffn, ln2_g[l], ln2_b[l])
    return h


_drawn_inputs = setup_inputs


def setup_inputs(seed=0):
    import zlib

    import numpy as np

    out = dict(_drawn_inputs(seed))
    spreads = {}
    factors = {'b_gate': 7.396,
     'lambda_q1': 3.446,
     'lambda_k1': 2.922,
     'lambda_q2': 33.45,
     'subln_g': 4.057,
     'pool_scale': 3.931,
     'ln2_g': 8.029,
     'ln2_b': 16.718}
    for name, (base, spread) in spreads.items():
        noise = np.random.default_rng([zlib.crc32(name.encode()), seed]).standard_normal(out[name].shape)
        drawn = base * np.exp(spread * noise) if base else spread * noise
        out[name] = __import__('jax').numpy.asarray(drawn.astype(out[name].dtype))
    for name, factor in factors.items():
        out[name] = (out[name] * factor).astype(out[name].dtype)
    return out
```

```python
from contextlib import ExitStack

import numpy as np

import concourse.bass as bass
from concourse import mybir

F32 = mybir.dt.float32
F32R = mybir.dt.float32r
I32 = mybir.dt.int32
U32 = mybir.dt.uint32
ACT = mybir.ActivationFunctionType
ALU = mybir.AluOpType
AX = mybir.AxisListType

P = 128
T = 1024
D = 1024
TT = T // P
DC = D // P
HALF = 512
H = 8
DH = 64
DV = 128
PG = 4
WINDOWS = (2, 4, 8, 16)
RH = 8
NK = 128
TOPK = 16
ALPHA = 2.0 ** 0.25
EPS = 1e-5
LAM_INIT = 0.2
SCALE = DH ** -0.5
MASK = -1.0e30
KB = 1024


class Place:

    def __init__(self, nc):
        self.nc = nc

    def __call__(self, name, kib, shape, dtype=F32):
        return self.nc.alloc_sbuf_tensor_at(name, shape, dtype, offset=int(BASE + kib * KB))


BASE = 16512


def split3(nc, out, lhs, rhs, pairs, first=True, last=True):
    n = 0
    for l, r in pairs:
        for a, b in ((0, 0), (0, 1), (1, 0)):
            ins = nc.tensor.matmul(out, l(lhs[a]), r(rhs[b]), start=first and n == 0,
                                   stop=last and n == 3 * len(pairs) - 1)
            n += 1
    return ins


WQKV = 3
KEYS = [(qt + 1) * P for qt in range(TT)]
CHUNKS = [(k + HALF - 1) // HALF for k in KEYS]
S_USES = [(w, qt, c) for qt in range(TT) for w in range(2) for c in range(CHUNKS[qt])]
AT_USES = [(qt, c) for qt in range(TT) for c in range(CHUNKS[qt])]


def transpose_uses(first, more):
    uses = []
    for s in range(TT if more else TT + 3):
        if s - 3 >= (0 if first else -3):
            uses.append(("o", s - 3, 0))
        if s == TT - 1 and more:
            uses.append(("v", 0, 0))
        if s - 1 >= (0 if first else -1) and s <= TT:
            uses += [("a", s - 1, c) for c in range(CHUNKS[s - 1])]
    if more:
        uses.append(("v", 1, 0))
    return uses


NS, NA = len(S_USES), len(AT_USES)
INIT = 2


def tr_at(h, use, first, more, splits=False):
    keep = (lambda uses: [x for x in uses if not splits or x[0] != "o"])
    own, middle, opening = (keep(transpose_uses(*kind)) for kind in ((first, more), (False, True), (True, True)))
    shift = INIT + len(opening) - len(middle)
    if first:
        i = INIT + own.index(use)
        return i, i % 2
    if use in own:
        i = shift + own.index(use)
    else:
        i = shift - len(middle) + middle.index((use[0], use[1] + TT, use[2]))
    return len(middle) * h + i, i % 2


def locate(h, tile):
    return (h, tile) if tile >= 0 else (h - 1, tile + TT)


def build_attention(nc, ctx, xT, w_in, lams, subln, const, oT_out, xT_hi, xT_lo, oT):
    at = Place(nc)
    x_raw = at("x_raw", 32, [P, DC, T])
    q = [[at(f"q{u}{s}", 96 + 16 * u + 4 * s, [P, T], F32R) for s in range(2)] for u in range(2)]
    k = [[at(f"k{u}{s}", 104 + 16 * u + 4 * s, [P, T], F32R) for s in range(2)] for u in range(2)]
    v = [[at(f"v{u}{s}", 128 + 8 * u + 4 * s, [P, TT, DV], F32R) for s in range(2)] for u in range(2)]
    w_raw = at("wa_raw", 144, [P, DC, P])
    w = [[at(f"wa{r}{s}", 148 + 8 * r + 4 * s, [P, DC, P], F32R) for s in range(2)] for r in range(2)]
    vT = at("vT", 164, [P, T])
    bias = at("bias", 168, [P, T])
    e = at("e", 172, [P, 2, T])
    a = [at("a0", 180, [P, T]), at("a1", 192, [P, T])]
    aT = [at(f"aT{s}", 184 + 4 * s, [P, 2, HALF], F32R) for s in range(2)]
    iota = at("iota_a", 192, [P, T], I32)
    ident, small = const
    osb = at("osb", 204 + 0.5, [P, DV])
    on = at("on", 204 + 1.0, [P, DV])
    sq = at("sq", 204 + 1.5, [P, DV])
    lam_in = at("lam_in", 196, [P, 4, DH])
    lam_t = at("lam_t", 197, [P, 2, DH])
    st = at("st_a", 204 + 2.0, [P, 32])
    mx, nmx, den, rden, ssq, rstd = (st[:, 0:4], st[:, 4:6], st[:, 6:8], st[:, 8:10], st[:, 10:11], st[:, 11:12])
    ms, mhalf, neglam, gain, le, lexp = (st[:, 12:13], st[:, 13:14], st[:, 14:15], st[:, 15:16], st[:, 16:18],
                                   st[:, 18:20])
    c2 = st[:, 20:21]

    s_ps = [ctx.enter_context(nc.psum_tensor(f"s_ps{i}", [P, HALF], F32)) for i in range(3)]
    j_ps = [ctx.enter_context(nc.psum_tensor(f"j_ps{i}", [P, HALF], F32)) for i in range(2)]
    t_ps = [ctx.enter_context(nc.psum_tensor(f"t_ps{i}", [P, HALF], F32)) for i in range(2)]
    o_ps = ctx.enter_context(nc.psum_tensor("o_ps", [P, DV], F32))

    def sem(name):
        return ctx.enter_context(nc.semaphore("a_" + name))

    x_in = [sem(f"x_in{c}") for c in range(DC)]
    x_hi, x_split = sem("x_hi"), sem("x_split")
    small_in, ready, tab = sem("small_in"), sem("consts_ready"), sem("table_steps")
    w_in_s, w_free, w_hi, w_split = (sem("w_in"), sem("w_raw_free"), sem("w_hi"), sem("w_split"))
    proj, qk_hi, qk_split, vT_copied, v_split = (sem("proj"), sem("qk_hi"), sem("qk_split"), sem("vT_copied"),
                                                 sem("v_split"))
    s_ready, s_free, mx_ready, e_ready, a_ready = (sem("s_ready"), sem("s_free"), sem("max_ready"), sem("e_ready"),
                                                   sem("a_ready"))
    tr_ready, tr_hi, tr_free = sem("tr_ready"), sem("tr_hi"), sem("tr_free")
    at_split, at_free = sem("aT_split"), sem("aT_free")
    o_free, ssq_ready, rstd_ready, on_ready = (sem("o_free"), sem("ssq_ready"),
                                                        sem("rstd_ready"), sem("on_ready"))
    pool_step, dve_step, act_step, bias_ready = sem("pool_step"), sem("dve_step"), sem("act_step"), sem("bias_ready")
    passed = sem("passed")

    block = ctx.enter_context(nc.Block())

    def heads(eng, body):
        body(0, 0, True, True)
        with eng.Fori(0, H // 2 - 1) as i:
            body(2 * i + 1, 1, False, True)
            body(2 * i + 2, 0, False, True)
        body(H - 1, 1, False, False)

    def steps_of(first, more):
        low = 0 if first else -TT
        for s in range(TT if more else TT + 3):
            yield s, *((s - d if s - d >= low and s - d < TT else None) for d in (3, 1, 2))

    @block.sync
    def _(sp):
        for c in range(DC):
            sp.dma_start(x_raw[:, c], xT[c * P:(c + 1) * P, :]).then_inc(x_in[c], 16)

        def load(n, blk):
            sp.wait_ge(w_free, n + 1)
            sp.dma_start(w_raw[:], w_in[blk]).then_inc(w_in_s, 16)

        for r in range(WQKV):
            load(r, r * H)
        with sp.Fori(1, H) as h:
            for r in range(WQKV):
                load(WQKV * h + r, r * H + h)

    @block.gpsimd
    def _(pool):
        nc.gpsimd.memset(ident[:], 0.0).then_inc(tab, 1)
        nc.gpsimd.iota(iota[:], [[1, T]], base=-(TT - 1) * P, channel_multiplier=-1).then_inc(tab, 1)
        nc.gpsimd.memset(mhalf, -0.5).then_inc(tab, 1)
        pool.wait_ge(tab, 3)
        nc.gpsimd.affine_select(out=ident[:], in_=ident[:], compare_op=ALU.not_equal, fill=1.0, base=0,
                                pattern=[[-1, P]], channel_multiplier=1).then_inc(tab, 1)
        nc.gpsimd.tensor_copy(bias[:], iota[:]).then_inc(tab, 1)
        pool.wait_ge(tab, 5)
        nc.gpsimd.affine_select(out=bias[:], in_=bias[:], compare_op=ALU.is_ge, fill=MASK, base=(TT - 1) * P,
                                pattern=[[-1, T]], channel_multiplier=1).then_inc(ready, 1)
        pool.sem_inc(w_free, 1)

        def split_weight(n, slot, wait):
            if wait:
                pool.wait_ge(proj, 2 * (n - 1))
            pool.wait_ge(w_in_s, 16 * (n + 1))
            pool.sem_inc(passed, 1)
            nc.gpsimd.tensor_copy(w[slot][0][:], w_raw[:]).then_inc(w_hi, 1)
            pool.wait_ge(w_hi, n + 1)
            nc.gpsimd.tensor_tensor(w[slot][1][:], w_raw[:], w[slot][0][:].bitcast(F32),
                                    ALU.subtract).then_inc(w_split, 1)
            pool.wait_ge(w_split, n + 1)
            pool.sem_inc(w_free, 1)

        for r in range(WQKV):
            split_weight(r, r % 2, r >= 2)

        def head(h, u, first, more):
            for s, _, _, product in steps_of(first, more):
                if more and s in (0, 1, 3):
                    r = (0, 1, 3).index(s)
                    split_weight(WQKV * (h + 1) + r, (WQKV * (u + 1) + r) % 2, True)
                if product is not None:
                    m = TT * h + product
                    pool.wait_ge(ssq_ready, m + 1)
                    pool.sem_inc(passed, 1)
                    nc.gpsimd.tensor_scalar(ms, ssq, 1.0 / DV, EPS, ALU.mult, ALU.add).then_inc(pool_step, 1)
                    pool.wait_ge(pool_step, m + 1)
                    nc.gpsimd.tensor_tensor(rstd, ms, mhalf, ALU.pow).then_inc(rstd_ready, 1)

        heads(pool, head)

    @block.scalar
    def _(act):
        for i, l in enumerate(lams):
            act.dma_start(lam_in[:, i, :], l.to_broadcast([P, DH])).then_inc(small_in, 16)
        act.dma_start(gain, subln).then_inc(small_in, 16)
        act.sem_inc(o_free, 1)
        act.sem_inc(at_free, 2)
        for c in range(DC):
            act.wait_ge(x_in[c], 16)
            nc.scalar.activation(xT_hi[:, c], x_raw[:, c], ACT.Copy).then_inc(x_hi, 1)
        act.wait_ge(dve_step, 2)
        nc.scalar.activation(lexp, le, ACT.Exp).then_inc(act_step, 1)

        def evac(h, j, u):
            act.wait_ge(proj, 6 * h + j + 1)
            if j < 4:
                dst = (q, q, k, k)[j][u][0]
                nc.scalar.activation(dst[:, (j % 2) * HALF:(j % 2 + 1) * HALF], j_ps[j % 2][:],
                                     ACT.Copy).then_inc(qk_hi, 1)
            else:
                nc.scalar.activation(vT[:, (j % 2) * HALF:(j % 2 + 1) * HALF], j_ps[j % 2][:],
                                     ACT.Copy).then_inc(vT_copied, 1)


        for j in range(6):
            evac(0, j, 0)
        for half in range(2):
            act.wait_ge(tr_ready, half + 1)
            nc.scalar.activation(v[0][0][:, 4 * half:4 * half + 4, :],
                                 t_ps[half][:].rearrange("p (t d) -> p t d", t=4), ACT.Copy).then_inc(tr_hi, 1)

        def head(h, u, first, more):
            def tr_split(use):
                i, bank = tr_at(h, use, first, more)
                act.wait_ge(tr_ready, i + 1)
                if use[0] == "v":
                    dst = v[1 - u][0][:, 4 * use[1]:4 * use[1] + 4, :]
                    nc.scalar.activation(dst, t_ps[bank][:].rearrange("p (t d) -> p t d", t=4),
                                         ACT.Copy).then_inc(tr_hi, 1)
                    return
                hh, qt = locate(h, use[1])
                i_a = AT_USES.index((qt, use[2]))
                n = min(HALF, KEYS[qt] - use[2] * HALF)
                act.wait_ge(at_free, NA * hh + i_a + 1)
                nc.scalar.activation(aT[0][:, i_a % 2, 0:n], t_ps[bank][:, 0:n], ACT.Copy).then_inc(tr_hi, 1)

            def take_output(tile):
                hh, qt = locate(h, tile)
                m = TT * hh + qt
                act.wait_ge(at_free, 2 + NA * hh + AT_USES.index((qt, CHUNKS[qt] - 1)) + 1)
                if not (first and tile == 0):
                    act.wait_ge(on_ready, m)
                nc.scalar.activation(osb[:], o_ps[:], ACT.Copy).then_inc(o_free, 1)
                act.wait_ge(o_free, m + 2)
                nc.scalar.activation(sq[:], osb[:], ACT.Square, accum_out=ssq).then_inc(ssq_ready, 1)

            def scale_output(tile):
                act.wait_ge(rstd_ready, TT * h + tile + 1)
                if not (first and tile == 0):
                    act.wait_ge(tr_ready, tr_at(h, ("o", tile - 1, 0), first, more)[0] + 1)
                nc.scalar.activation(on[:], osb[:], ACT.Copy, scale=rstd).then_inc(on_ready, 1)

            for s, turned, transposed, product in steps_of(first, more):
                if s < TT:
                    act.wait_ge(mx_ready, TT * h + s + 1)
                    for wh in range(2):
                        nc.scalar.activation(e[:, wh, 0:KEYS[s]], e[:, wh, 0:KEYS[s]], ACT.Exp,
                                             bias=nmx[:, wh:wh + 1], accum_out=den[:, wh:wh + 1]).then_inc(e_ready, 1)
                if turned is not None:
                    scale_output(turned)
                if more and 1 <= s < 7:
                    evac(h + 1, s - 1, 1 - u)
                if product is not None:
                    take_output(product)
                if more and s == TT - 1:
                    tr_split(("v", 0, 0))
                if transposed is not None:
                    for c in range(CHUNKS[transposed]):
                        tr_split(("a", transposed, c))
            if more:
                tr_split(("v", 1, 0))

        heads(act, head)

    @block.vector
    def _(dve):
        steps = [0]

        def then(ins):
            steps[0] += 1
            ins.then_inc(dve_step, 1)
            dve.wait_ge(dve_step, steps[0])

        dve.sem_inc(s_free, 3)
        dve.sem_inc(tr_free, 2)
        dve.sem_inc(a_ready, 1)
        dve.wait_ge(small_in, 16 * 5)
        for i in range(2):
            then(nc.vector.tensor_tensor_reduce(lam_t[:, i, :], lam_in[:, 2 * i, :], lam_in[:, 2 * i + 1, :], 1.0, 0.0,
                                                ALU.mult, ALU.add, le[:, i:i + 1]))
        then(nc.vector.tensor_scalar(gain, gain, 1.0 - LAM_INIT, None, ALU.mult))
        for c in range(DC):
            dve.wait_ge(x_hi, c + 1)
            nc.vector.tensor_tensor(xT_lo[:, c], x_raw[:, c], xT_hi[:, c].bitcast(F32), ALU.subtract)\
                .then_inc(x_split, 1)
        dve.wait_ge(act_step, 1)
        then(nc.vector.tensor_tensor(neglam, lexp[:, 1:2], lexp[:, 0:1], ALU.subtract))
        then(nc.vector.tensor_scalar(neglam, neglam, -LAM_INIT, None, ALU.add))
        dve.wait_ge(ready, 1)
        then(nc.vector.tensor_scalar(bias[:], bias[:], 1.0 / SCALE, None, ALU.mult))
        setup = steps[0]

        def low(h, j, u):
            dve.wait_ge(qk_hi, 4 * h + j + 1)
            dst = (q, q, k, k)[j][u]
            half = slice((j % 2) * HALF, (j % 2 + 1) * HALF)
            nc.vector.tensor_tensor(dst[1][:, half], j_ps[j % 2][:], dst[0][:, half].bitcast(F32),
                                    ALU.subtract).then_inc(qk_split, 1)

        for j in range(4):
            low(0, j, 0)
        for half in range(2):
            dve.wait_ge(tr_hi, half + 1)
            part = slice(4 * half, 4 * half + 4)
            nc.vector.tensor_tensor(v[0][1][:, part, :], t_ps[half][:].rearrange("p (t d) -> p t d", t=4),
                                    v[0][0][:, part, :].bitcast(F32), ALU.subtract).then_inc(tr_free, 1)

        SM = 3
        HM = TT * SM + 1

        def head(h, u, first, more):
            def tr_low(use):
                i, bank = tr_at(h, use, first, more)
                ps = t_ps[bank]
                if use[0] == "o":
                    hh, qt = locate(h, use[1])
                    dve.wait_ge(tr_ready, i + 1)
                    nc.vector.tensor_scalar(oT[:, hh, qt * P:(qt + 1) * P], ps[:, 0:P], gain, None,
                                            ALU.mult).then_inc(tr_free, 1)
                    return
                dve.wait_ge(tr_hi, tr_at(h, use, first, more, True)[0] + 1)
                if use[0] == "v":
                    part = slice(4 * use[1], 4 * use[1] + 4)
                    nc.vector.tensor_tensor(v[1 - u][1][:, part, :], ps[:].rearrange("p (t d) -> p t d", t=4),
                                            v[1 - u][0][:, part, :].bitcast(F32), ALU.subtract).then_inc(tr_free, 1)
                    return
                qt = locate(h, use[1])[1]
                i_a = AT_USES.index((qt, use[2]))
                n = min(HALF, KEYS[qt] - use[2] * HALF)
                nc.vector.tensor_tensor(aT[1][:, i_a % 2, 0:n], ps[:, 0:n], aT[0][:, i_a % 2, 0:n].bitcast(F32),
                                        ALU.subtract).then_inc(tr_free, 1)

            at_step = setup + HM * h
            nc.vector.tensor_scalar(bias[:], bias[:], 0.5, None, ALU.mult).then_inc(dve_step, 1)
            dve.wait_ge(dve_step, at_step + 1)
            def logits(qt):
                m = TT * h + qt
                dve.wait_ge(a_ready, m + 1)
                for wh in range(2):
                    for c in range(CHUNKS[qt]):
                        i = S_USES.index((wh, qt, c))
                        n = min(HALF, KEYS[qt] - c * HALF)
                        dve.wait_ge(s_ready, NS * h + i + 1)
                        dve.sem_inc(passed, 1)
                        start = c * HALF + (TT - 1 - qt) * P
                        nc.vector.tensor_tensor_reduce(e[:, wh, c * HALF:c * HALF + n], s_ps[i % 3][:, 0:n],
                                                       bias[:, start:start + n], SCALE, -3.0e38, ALU.add, ALU.max,
                                                       mx[:, 2 * wh + c:2 * wh + c + 1]).then_inc(s_free, 1)
                i = S_USES.index((1, qt, CHUNKS[qt] - 1))
                dve.wait_ge(s_free, 3 + NS * h + i + 1)
                nc.vector.tensor_reduce(nmx, mx.rearrange("p (w c) -> p w c", w=2)[:, :, 0:CHUNKS[qt]], AX.X, ALU.max,
                                        negate=True).then_inc(mx_ready, 1)

            def combine(qt):
                base = at_step + 1 + SM * qt
                dve.wait_ge(e_ready, 2 * (TT * h + qt) + 2)
                nc.vector.reciprocal(rden, den).then_inc(dve_step, 1)
                dve.wait_ge(dve_step, base + 1)
                nc.vector.tensor_scalar(c2, rden[:, 1:2], neglam, None, ALU.mult).then_inc(dve_step, 1)
                dve.wait_ge(dve_step, base + 2)
                n = KEYS[qt]
                nc.vector.tensor_scalar(e[:, 1, 0:n], e[:, 1, 0:n], c2, None, ALU.mult).then_inc(dve_step, 1)
                dve.wait_ge(dve_step, base + 3)
                nc.vector.scalar_tensor_tensor(a[qt % 2][:, 0:n], e[:, 0, 0:n], rden[:, 0:1], e[:, 1, 0:n],
                                               ALU.mult, ALU.add).then_inc(a_ready, 1)

            for s, turned, transposed, _ in steps_of(first, more):
                if s < TT:
                    logits(s)
                    combine(s)
                if more and 1 <= s < 5:
                    low(h + 1, s - 1, 1 - u)
                if turned is not None:
                    tr_low(("o", turned, 0))
                if more and s == TT - 1:
                    tr_low(("v", 0, 0))
                if transposed is not None:
                    for c in range(CHUNKS[transposed]):
                        tr_low(("a", transposed, c))
            if more:
                tr_low(("v", 1, 0))

        heads(dve, head)

    @block.tensor
    def _(pe):
        def project(h, j, u):
            r, half = j // 2, j % 2
            if half == 0:
                pe.wait_ge(w_split, WQKV * h + r + 1)
            if not (isinstance(h, int) and h == 0 and j < 2):
                if j < 2:
                    pe.wait_ge(vT_copied, 2 * h - 1 + j)
                else:
                    pe.wait_ge(qk_split, 4 * h + j - 1)
            slot = (WQKV * u + r) % 2
            ins = split3(nc, j_ps[half][:], w[slot], (xT_hi, xT_lo),
                         [(lambda t, c=c: t[:, c, :], lambda t, c=c: t[:, c, half * HALF:(half + 1) * HALF])
                          for c in range(DC)])
            ins.then_inc(proj, 1)

        def v_transposes(h, half, bank):
            pe.wait_ge(vT_copied, 2 * h + half + 1)
            for b in range(4):
                t = 4 * half + b
                ins = nc.tensor.transpose(t_ps[bank][:, b * P:(b + 1) * P], vT[:, t * P:(t + 1) * P], ident[:])
            ins.then_inc(tr_ready, 1)

        pe.wait_ge(x_split, DC)
        pe.wait_ge(tab, 5)
        for j in range(6):
            project(0, j, 0)
        for half in range(2):
            pe.wait_ge(tr_free, half + 1)
            v_transposes(0, half, half)

        def head(h, u, first, more):
            def scores(qt):
                if qt == 0:
                    pe.wait_ge(qk_split, 4 * h + 4)
                for wh in range(2):
                    rows = slice(wh * DH, (wh + 1) * DH)
                    for c in range(CHUNKS[qt]):
                        i = S_USES.index((wh, qt, c))
                        n = min(HALF, KEYS[qt] - c * HALF)
                        pe.wait_ge(s_free, NS * h + i + 1)
                        split3(nc, s_ps[i % 3][:, 0:n], q[u], k[u],
                               [(lambda t: t[rows, qt * P:(qt + 1) * P], lambda t: t[rows, c * HALF:c * HALF + n])]
                               ).then_inc(s_ready, 1)

            def turn(use):
                i, bank = tr_at(h, use, first, more)
                pe.wait_ge(tr_free, i + 1)
                if use[0] == "v":
                    v_transposes(h + 1, use[1], bank)
                elif use[0] == "o":
                    pe.wait_ge(on_ready, TT * h + use[1] + 1)
                    nc.tensor.transpose(t_ps[bank][:, 0:P], on[:], ident[:]).then_inc(tr_ready, 1)
                else:
                    qt = locate(h, use[1])[1]
                    if use[2] == 0:
                        pe.wait_ge(a_ready, 1 + TT * h + use[1] + 1)
                    for b in range(min(4, qt + 1 - 4 * use[2])):
                        start = use[2] * HALF + b * P
                        ins = nc.tensor.transpose(t_ps[bank][:, b * P:(b + 1) * P], a[qt % 2][:, start:start + P],
                                                  ident[:])
                    ins.then_inc(tr_ready, 1)

            def values(tile):
                hh, qt = locate(h, tile)
                pe.wait_ge(o_free, TT * hh + qt + 1)
                for c in range(CHUNKS[qt]):
                    i_a = AT_USES.index((qt, c))
                    pe.wait_ge(tr_free, 2 + tr_at(h, ("a", tile, c), first, more)[0] + 1)
                    blocks = range(min(4, qt + 1 - 4 * c))
                    ins = split3(nc, o_ps[:], aT, v[u if tile >= 0 else 1 - u],
                                 [(lambda t, b=b: t[:, i_a % 2, b * P:(b + 1) * P],
                                   lambda t, b=b: t[:, 4 * c + b, :]) for b in blocks],
                                 first=c == 0, last=c == CHUNKS[qt] - 1)
                    ins.then_inc(at_free, 1)

            for s, turned, transposed, product in steps_of(first, more):
                if s < TT:
                    scores(s)
                if more and 1 <= s < 7:
                    project(h + 1, s - 1, 1 - u)
                if product is not None:
                    values(product)
                if turned is not None:
                    turn(("o", turned, 0))
                if more and s == TT - 1:
                    turn(("v", 0, 0))
                if transposed is not None:
                    for c in range(CHUNKS[transposed]):
                        turn(("a", transposed, c))
            if more:
                turn(("v", 1, 0))

        heads(pe, head)


CA, CP = H, PG
PAD = 16


def build_branches(nc, ctx, w_in, pool_w, pool_scale, b_gate, w_branch, xT, oT, merged):
    at = Place(nc)
    pad = [at(f"pad{i}", 96 + 5 * i, [P, PAD + T]) for i in range(3)]
    pooled = [at(f"pooled{s}", 111 + 4 * s, [P, T], F32R) for s in range(2)]
    pw_raw = at("pw_raw", 119, [P, PG, P])
    pw = [at(f"pw{s}", 121 + 2 * s, [P, PG, P], F32R) for s in range(2)]
    count = at("count", 125, [P, PAD])
    icount = at("icount", 125.25, [P, PAD], I32)
    gates = at("gates", 96, [P, 2 * DC, T])
    pm_all = at("pm", 160, [P, PG, T])
    pm = [at("pm_hi", 32, [P, PG, T], F32R), at("pm_lo", 160, [P, PG, T], F32R)]
    w_raw = at("wb_raw", 176, [P, DC, P])
    w = [[at(f"wb{r}{s}", 180 + 8 * r + 4 * s, [P, DC, P], F32R) for s in range(2)] for r in range(2)]
    wc_raw = at("wc_raw", 48, [P, CA + CP, P])
    wc = [[at(f"wc{r}{s}", 176 + 12 * r + 6 * s, [P, CA + CP, P], F32R) for s in range(2)] for r in range(2)]
    o = [at("oT_hi", 0, [P, H, T], F32R), at("oT_lo", 64, [P, H, T], F32R)]
    branch = at("branch", 54, [P, 2, HALF])
    bg = at("bg", 206.5, [P, 2 * DC])
    psc = at("psc", 206.75, [P, PG])
    ps = [ctx.enter_context(nc.psum_tensor(f"b_ps{i}", [P, HALF], F32)) for i in range(8)]

    def sem(name):
        return ctx.enter_context(nc.semaphore("b_" + name))

    small_in, table, pw_hi = sem("small_in"), sem("table"), sem("pw_hi")
    w_raw_in, w_free, w_hi, w_split, unit = (sem("w_raw_in"), sem("w_free"), sem("w_hi"), sem("w_split"),
                                             sem("projected"))
    p_copied, p_step, pooled_hi, pooled_split, pm_unit, pm_scaled = (
        sem("p_copied"), sem("p_step"), sem("pooled_hi"), sem("pooled_split"), sem("pm_unit"), sem("pm_scaled"))
    gate_done = sem("gate_done")
    c_raw_in, c_free, c_hi, c_split, c_unit = (sem("c_raw_in"), sem("c_free"), sem("c_hi"), sem("c_split"),
                                               sem("branches"))
    o_hi, o_split, gated = sem("o_hi"), sem("o_split"), sem("gated")
    block = ctx.enter_context(nc.Block())
    NP = PG
    NG = 2 * DC
    FIRST = WQKV * H

    @block.sync
    def _(sp):
        sp.dma_start(pw_raw[:], pool_w).then_inc(small_in, 16)
        sp.dma_start(bg[:], b_gate).then_inc(small_in, 16)
        sp.dma_start(psc[:], pool_scale).then_inc(small_in, 16)
        with sp.Fori(0, NP + NG) as n:
            sp.wait_ge(w_free, n + 1)
            sp.dma_start(w_raw[:], w_in[n + FIRST]).then_inc(w_raw_in, 16)
        with sp.Fori(0, DC) as n:
            sp.wait_ge(c_free, n + 1)
            sp.dma_start(wc_raw[:], w_branch[n]).then_inc(c_raw_in, 16)

    @block.gpsimd
    def _(pool):
        nc.gpsimd.iota(icount[:], [[1, PAD]], base=1, channel_multiplier=0).then_inc(table, 1)
        nc.gpsimd.memset(pad[0][:, 0:PAD], 0.0).then_inc(table, 1)
        nc.gpsimd.memset(pad[1][:, 0:PAD], 0.0).then_inc(table, 1)
        nc.gpsimd.memset(pad[2][:, 0:PAD], 0.0).then_inc(table, 1)
        pool.sem_inc(w_free, 1)

        def low(n, r):
            pool.wait_ge(w_hi, n + 1)
            nc.gpsimd.tensor_tensor(w[r][1][:], w_raw[:], w[r][0][:].bitcast(F32), ALU.subtract).then_inc(w_split, 1)
            pool.wait_ge(w_split, n + 1)
            pool.sem_inc(w_free, 1)

        with pool.Fori(0, (NP + NG) // 2) as i:
            low(2 * i, 0)
            low(2 * i + 1, 1)
        pool.wait_ge(unit, 2 * (NP + NG))
        pool.sem_inc(c_free, 1)
        with pool.Fori(0, DC // 2) as i:
            for r in range(2):
                n = 2 * i + r
                pool.wait_ge(c_hi, n + 1)
                nc.gpsimd.tensor_tensor(wc[r][1][:], wc_raw[:], wc[r][0][:].bitcast(F32),
                                        ALU.subtract).then_inc(c_split, 1)
                pool.wait_ge(c_split, n + 1)
                pool.sem_inc(c_free, 1)

    @block.scalar
    def _(act):
        def high(n, r, wait):
            act.wait_ge(w_raw_in, 16 * (n + 1))
            if wait:
                act.wait_ge(unit, 2 * (n - 1))
            nc.scalar.activation(w[r][0][:], w_raw[:], ACT.Copy).then_inc(w_hi, 1)

        act.sem_inc(gate_done, 4)
        act.wait_ge(small_in, 16 * 3)
        nc.scalar.activation(pw[0][:], pw_raw[:], ACT.Copy).then_inc(pw_hi, 1)
        high(0, 0, False)
        high(1, 1, False)
        for g in range(PG):
            for half in range(2):
                act.wait_ge(unit, 2 * g + half + 1)
                if g and not half:
                    act.wait_ge(p_step, 8 * g)
                nc.scalar.activation(pad[0][:, PAD + half * HALF:PAD + (half + 1) * HALF], ps[half][:],
                                     ACT.Copy).then_inc(p_copied, 1)
            high(g + 2, g % 2, True)
            act.wait_ge(p_step, 8 * (g + 1))
            if g:
                act.wait_ge(pm_unit, 2 * g)
            nc.scalar.activation(pooled[0][:], pad[1][:, PAD:], ACT.Copy).then_inc(pooled_hi, 1)
            for half in range(2):
                act.wait_ge(pm_unit, 2 * g + half + 1)
                nc.scalar.activation(pm_all[:, g, half * HALF:(half + 1) * HALF], ps[2 + half][:], ACT.Copy,
                                     scale=psc[:, g:g + 1]).then_inc(pm_scaled, 1)

        def gate(i, r):
            for half in range(2):
                act.wait_ge(unit, 2 * (i + NP) + half + 1)
                nc.scalar.activation(gates[:, i, half * HALF:(half + 1) * HALF], ps[4 + 2 * r + half][:], ACT.Sigmoid,
                                     bias=bg[:, bass.ds(i, 1)]).then_inc(gate_done, 1)

        with act.Fori(0, NG // 2 - 1) as i:
            for r in range(2):
                gate(2 * i + r, r)
                high(2 * i + r + NP + 2, r, True)
        gate(NG - 2, 0)
        gate(NG - 1, 1)
        for c in range(H):
            nc.scalar.activation(o[0][:, c], oT[:, c], ACT.Copy).then_inc(o_hi, 1)
        for c in range(PG):
            nc.scalar.activation(pm[0][:, c], pm_all[:, c], ACT.Copy).then_inc(o_hi, 1)

        def branch_high(n, r, wait):
            act.wait_ge(c_raw_in, 16 * (n + 1))
            if wait:
                act.wait_ge(c_unit, 4 * (n - 1))
            nc.scalar.activation(wc[r][0][:], wc_raw[:], ACT.Copy).then_inc(c_hi, 1)

        branch_high(0, 0, False)
        branch_high(1, 1, False)
        with act.Fori(1, DC // 2) as i:
            branch_high(2 * i, 0, True)
            branch_high(2 * i + 1, 1, True)

    @block.vector
    def _(dve):
        dve.wait_ge(table, 4)
        nc.vector.tensor_copy(count[:], icount[:]).then_inc(table, 1)
        dve.wait_ge(table, 5)
        nc.vector.reciprocal(count[:], count[:]).then_inc(table, 1)
        dve.wait_ge(table, 6)
        dve.wait_ge(pw_hi, 1)
        nc.vector.tensor_tensor(pw[1][:], pw_raw[:], pw[0][:].bitcast(F32), ALU.subtract).then_inc(pw_hi, 1)
        for g, window in enumerate(WINDOWS):
            step = 8 * g

            def then(ins, n):
                ins.then_inc(p_step, n)
                return n

            dve.wait_ge(p_copied, 2 * g + 2)
            if g:
                dve.wait_ge(pooled_hi, g)
            src = 0
            for level in range(g + 1):
                dst = 1 + (level + g + 1) % 2
                lag = 1 << level
                step += then(nc.vector.tensor_tensor(pad[dst][:, PAD:], pad[src][:, PAD:],
                                                     pad[src][:, PAD - lag:PAD + T - lag], ALU.add), 1)
                dve.wait_ge(p_step, step)
                src = dst
            dst = 3 - src
            step += then(nc.vector.tensor_tensor(pad[dst][:, PAD:PAD + window], pad[src][:, PAD:PAD + window],
                                                 count[:, 0:window], ALU.mult), 1)
            dve.wait_ge(p_step, step)
            step += then(nc.vector.tensor_tensor(pad[dst][:, PAD:PAD + window], pad[dst][:, PAD:PAD + window],
                                                 pad[0][:, PAD:PAD + window], ALU.subtract), 1)
            nc.vector.scalar_tensor_tensor(pad[dst][:, PAD + window:], pad[src][:, PAD + window:], 1.0 / window,
                                           pad[0][:, PAD + window:], ALU.mult,
                                           ALU.subtract).then_inc(p_step, 8 * (g + 1) - step)
            dve.wait_ge(pooled_hi, g + 1)
            nc.vector.tensor_tensor(pooled[1][:], pad[dst][:, PAD:], pooled[0][:].bitcast(F32),
                                    ALU.subtract).then_inc(pooled_split, 1)
            dve.wait_ge(pooled_split, g + 1)
        for c in range(H):
            dve.wait_ge(o_hi, c + 1)
            nc.vector.tensor_tensor(o[1][:, c], oT[:, c], o[0][:, c].bitcast(F32), ALU.subtract).then_inc(o_split, 1)
        for c in range(PG):
            dve.wait_ge(o_hi, H + c + 1)
            nc.vector.tensor_tensor(pm[1][:, c], pm_all[:, c], pm[0][:, c].bitcast(F32),
                                    ALU.subtract).then_inc(o_split, 1)
        dve.wait_ge(gate_done, 4 + 2 * NG)
        dve.sem_inc(gated, 12)
        with dve.Fori(0, DC // 2) as i:
            for r in range(2):
                n = 2 * i + r
                for half in range(2):
                    cols = slice(half * HALF, (half + 1) * HALF)
                    dve.wait_ge(c_unit, 4 * n + half + 1)
                    nc.vector.tensor_tensor(gates[:, n, cols], gates[:, n, cols], ps[4 * r + half][:],
                                            ALU.mult).then_inc(gated, 1)
                for half in range(2):
                    cols = slice(half * HALF, (half + 1) * HALF)
                    dve.wait_ge(c_unit, 4 * n + 2 + half + 1)
                    nc.vector.tensor_tensor(branch[:, half], gates[:, n + DC, cols], ps[4 * r + 2 + half][:],
                                            ALU.mult).then_inc(gated, 1)
                dve.wait_ge(gated, 12 + 6 * n + 4)
                for half in range(2):
                    cols = slice(half * HALF, (half + 1) * HALF)
                    nc.vector.tensor_tensor(merged[:, n, cols], gates[:, n, cols], branch[:, half],
                                            ALU.add).then_inc(gated, 1)
                dve.wait_ge(gated, 12 + 6 * n + 6)

    @block.tensor
    def _(pe):
        def product(out, lhs, rhs, half, chunks):
            return split3(nc, out, lhs, rhs,
                          [(lambda t, c=c: t[:, c[0], :], lambda t, c=c: t[:, c[1], half * HALF:(half + 1) * HALF])
                           for c in chunks])

        def pool_product(g):
            pe.wait_ge(pw_hi, 2)
            pe.wait_ge(pooled_split, g + 1)
            for half in range(2):
                if g:
                    pe.wait_ge(pm_scaled, 2 * g - 1 + half)
                split3(nc, ps[2 + half][:], pw, pooled,
                       [(lambda t: t[:, g, :], lambda t: t[:, half * HALF:(half + 1) * HALF])]).then_inc(pm_unit, 1)

        for g in range(PG):
            for half in range(2):
                if not half:
                    pe.wait_ge(w_split, g + 1)
                if g:
                    pe.wait_ge(p_copied, 2 * g - 1 + half)
                product(ps[half][:], w[g % 2], xT, half, [(c, c) for c in range(DC)]).then_inc(unit, 1)
            if g:
                pool_product(g - 1)
        pool_product(PG - 1)
        with pe.Fori(0, NG // 2) as i:
            for r in range(2):
                n = 2 * i + r
                pe.wait_ge(w_split, n + NP + 1)
                for half in range(2):
                    pe.wait_ge(gate_done, 2 * n + half + 1)
                    product(ps[4 + 2 * r + half][:], w[r], xT, half, [(c, c) for c in range(DC)]).then_inc(unit, 1)
        pe.wait_ge(gate_done, 4 + 2 * NG)
        pe.wait_ge(o_split, CA + CP)
        with pe.Fori(0, DC // 2) as i:
            for r in range(2):
                n = 2 * i + r
                pe.wait_ge(c_split, n + 1)
                pe.wait_ge(gated, 6 * n + 4)
                for half in range(2):
                    product(ps[4 * r + half][:], wc[r], o, half, [(c, c) for c in range(CA)]).then_inc(c_unit, 1)
                for half in range(2):
                    product(ps[4 * r + 2 + half][:], wc[r], pm, half,
                            [(CA + c, c) for c in range(CP)]).then_inc(c_unit, 1)


def lagged(eng, front, back):
    front(0, 0)
    with eng.Fori(0, TT // 2 - 1) as i:
        for u in (1, 0):
            n = 2 * i + 2 - u
            front(n, u)
            back(n - 1, 1 - u)
    front(TT - 1, 1)
    back(TT - 2, 0)
    back(TT - 1, 1)


def nothing(n, u):
    pass


def build_first_norm(nc, ctx, x, w_out, ln_g, ln_b, ident, merged, yT, y_scr):
    at = Place(nc)
    w_raw = at("wo_raw", 0, [P, DC, D])
    w = [at("wo_hi", 32, [P, DC, D], F32R), at("wo_lo", 0, [P, DC, D], F32R)]
    m = [[at(f"mt{u}{s}", 128 + 8 * u + 4 * s, [P, DC, P], F32R) for s in range(2)] for u in range(2)]
    xs = at("xs", 144, [P, 2, D])
    z = at("z", 152, [P, D])
    yn = at("yn", 156, [P, D])
    y = at("y", 160, [P, 2, D])
    gb = at("gb", 168, [P, 2, D])
    st = at("st_c", 206.5, [P, 20])
    stats, mv, rstd, nmr, var, mhalf = (st[:, 0:12], st[:, 12:14], st[:, 14:15], st[:, 15:16], st[:, 16:17],
                                        st[:, 17:18])
    mix = [[ctx.enter_context(nc.psum_tensor(f"mix{u}{h}", [P, HALF], F32)) for h in range(2)] for u in range(2)]
    t_ps = [ctx.enter_context(nc.psum_tensor(f"ct_ps{i}", [P, HALF], F32)) for i in range(2)]

    def sem(name):
        return ctx.enter_context(nc.semaphore("c_" + name))

    w_in_s = [sem(f"w_in{c}") for c in range(DC)]
    w_hi, w_split, gb_in, const = sem("w_hi"), sem("w_split"), sem("gb_in"), sem("const")
    x_in, m_hi, m_split, mixed, z_ready = sem("x_in"), sem("m_hi"), sem("m_split"), sem("mixed"), sem("z_ready")
    stat_step, rstd_ready, nmr_ready, yn_ready = sem("stat_step"), sem("rstd_ready"), sem("nmr_ready"), sem("yn_ready")
    y_scaled, y_ready, y_out, y_free = sem("y_scaled"), sem("y_ready"), sem("y_out"), sem("y_free")
    tr_ready, tr_copied, passed = sem("tr_ready"), sem("tr_copied"), sem("passed")
    block = ctx.enter_context(nc.Block())

    @block.sync
    def _(sp):
        for c in range(DC):
            sp.dma_start(w_raw[:, c], w_out[c * P:(c + 1) * P, :]).then_inc(w_in_s[c], 16)
        sp.dma_start(gb[:, 0], ln_g.to_broadcast([P, D])).then_inc(gb_in, 16)
        sp.dma_start(gb[:, 1], ln_b.to_broadcast([P, D])).then_inc(gb_in, 16)
        sp.sem_inc(y_free, 2)

        def front(n, u):
            sp.wait_ge(z_ready, 2 * n + 2)
            sp.dma_start(xs[:, u], x[n]).then_inc(x_in, 16)
            sp.wait_ge(x_in, 16 * (n + 1))

        def back(n, u):
            sp.wait_ge(y_ready, n + 1)
            sp.dma_start(y_scr[n], y[:, u]).then_inc(y_out, 16)
            sp.wait_ge(y_out, 16 * (n + 1))
            sp.sem_inc(y_free, 1)

        lagged(sp, front, back)

    @block.gpsimd
    def _(pool):
        nc.gpsimd.memset(mhalf, -0.5).then_inc(const, 1)
        pool.wait_ge(const, 1)

        def back(n, u):
            pool.wait_ge(stat_step, 4 * n + 4)
            nc.gpsimd.tensor_tensor(rstd, var, mhalf, ALU.pow).then_inc(rstd_ready, 1)

        lagged(pool, nothing, back)

    @block.scalar
    def _(act):
        act.sem_inc(yn_ready, 1)
        act.sem_inc(tr_copied, 2)
        for c in range(DC):
            act.wait_ge(w_in_s[c], 16)
            nc.scalar.activation(w[0][:, c], w_raw[:, c], ACT.Copy).then_inc(w_hi, 1)

        def front(n, u):
            act.wait_ge(mixed, 2 * n + 2)
            nc.scalar.activation(m[u][0][:], merged[:, :, bass.ds(n * P, P)], ACT.Copy).then_inc(m_hi, 1)

        def back(n, u):
            act.wait_ge(nmr_ready, n + 1)
            act.wait_ge(y_scaled, n + 1)
            nc.scalar.activation(yn[:], z[:], ACT.Identity, scale=rstd, bias=nmr).then_inc(yn_ready, 1)
            for half in range(2):
                act.wait_ge(tr_ready, 2 * n + half + 1)
                nc.scalar.activation(yT[:, 4 * half:4 * half + 4, bass.ds(n * P, P)],
                                     t_ps[half][:].rearrange("p (c t) -> p c t", c=4),
                                     ACT.Copy).then_inc(tr_copied, 1)

        lagged(act, front, back)

    @block.vector
    def _(dve):
        dve.sem_inc(z_ready, 4)
        dve.sem_inc(y_scaled, 1)
        for c in range(DC):
            dve.wait_ge(w_hi, c + 1)
            nc.vector.tensor_tensor(w[1][:, c], w_raw[:, c], w[0][:, c].bitcast(F32),
                                    ALU.subtract).then_inc(w_split, 1)
        dve.wait_ge(gb_in, 32)

        def front(n, u):
            dve.wait_ge(m_hi, n + 1)
            nc.vector.tensor_tensor(m[u][1][:], merged[:, :, bass.ds(n * P, P)], m[u][0][:].bitcast(F32),
                                    ALU.subtract).then_inc(m_split, 1)

        def back(n, u):
            dve.wait_ge(x_in, 16 * (n + 1))
            dve.wait_ge(yn_ready, n + 1)
            for half in range(2):
                cols = slice(half * HALF, (half + 1) * HALF)
                dve.wait_ge(mixed, 4 + 2 * n + half + 1)
                nc.vector.scalar_tensor_tensor(z[:, cols], xs[:, u, cols], ALPHA, mix[u][half][:], ALU.mult,
                                               ALU.add).then_inc(z_ready, 1)
            for half in range(2):
                dve.wait_ge(z_ready, 4 + 2 * n + half + 1)
                nc.vector.bn_stats(stats[:, 6 * half:6 * half + 6],
                                   z[:, half * HALF:(half + 1) * HALF]).then_inc(stat_step, 1)
            dve.wait_ge(stat_step, 4 * n + 2)
            dve.sem_inc(passed, 1)
            nc.vector.bn_aggr(mv, stats).then_inc(stat_step, 1)
            dve.wait_ge(stat_step, 4 * n + 3)
            nc.vector.tensor_scalar(var, mv[:, 1:2], EPS, None, ALU.add).then_inc(stat_step, 1)
            dve.wait_ge(rstd_ready, n + 1)
            nc.vector.tensor_scalar(nmr, mv[:, 0:1], rstd, -1.0, ALU.mult, ALU.mult).then_inc(nmr_ready, 1)
            dve.wait_ge(y_free, n + 1)
            dve.wait_ge(yn_ready, n + 2)
            nc.vector.tensor_tensor(y[:, u], yn[:], gb[:, 0], ALU.mult).then_inc(y_scaled, 1)
            dve.wait_ge(y_scaled, n + 2)
            nc.vector.tensor_tensor(y[:, u], y[:, u], gb[:, 1], ALU.add).then_inc(y_ready, 1)

        lagged(dve, front, back)

    @block.tensor
    def _(pe):
        pe.sem_inc(mixed, 4)
        pe.wait_ge(w_split, DC)

        def front(n, u):
            pe.wait_ge(m_split, n + 1)
            pe.wait_ge(z_ready, 2 * n + 2)
            for half in range(2):
                split3(nc, mix[u][half][:], m[u], w,
                       [(lambda t, c=c: t[:, c, :], lambda t, c=c: t[:, c, half * HALF:(half + 1) * HALF])
                        for c in range(DC)]).then_inc(mixed, 1)

        def back(n, u):
            pe.wait_ge(y_ready, n + 1)
            for half in range(2):
                pe.wait_ge(tr_copied, 2 * n + half + 1)
                for b in range(4):
                    c = 4 * half + b
                    ins = nc.tensor.transpose(t_ps[half][:, b * P:(b + 1) * P], y[:, u, c * P:(c + 1) * P], ident[:])
                ins.then_inc(tr_ready, 1)

        lagged(pe, front, back)


HP = 2 * RH
CAND = TOPK * TOPK
HS = 4
TB = 32
GT = 4
NB = P // TB
NEG = -3.0e38


def build_retrieval(nc, ctx, wqT, keysT, ident, yT, g_scr):
    at = Place(nc)
    km = at("km", 0, [P, DC, HP * NK])
    wq = at("wq", 96, [P, 2, D])
    kT = at("kT", 104, [P, HP, NK])
    gblock = at("gblock", 96, [P, 2, NK, TB])
    ytile = at("ytile", 128, [P, DC, P])
    s = at("s", 136, [P, HP, NK])
    s2 = at("s2", 144, [P, HP, NK])
    cand = at("cand", 152, [P, RH, CAND])
    cand2 = at("cand2", 160, [P, RH, CAND])
    hot = at("hot", 168, [P, RH, TOPK, TOPK])
    rows = at("rows", 176, [P, HS, GT, P])
    cols = at("cols", 195, [P, HS, GT, P])
    top = at("top", 184, [P, RH, 2, TOPK])
    topi = at("topi", 185, [P, HP, TOPK], U32)
    topf = at("topf", 186, [P, RH, 2, TOPK])
    best = at("best", 187, [P, RH, TOPK])
    besti = at("besti", 187.5, [P, RH, TOPK], U32)
    ab = at("ab", 188, [P, 2, RH, TOPK], U32)
    abf = at("abf", 189, [P, 2, RH, TOPK])
    rcg = at("rcg", 190, [P, 3, P])
    rcgT = at("rcgT", 191.5, [P, 3, P])
    iota_i = at("iota_i", 193, [P, P], I32)
    iota = at("iota_r", 193.5, [P, P])
    esum = at("esum", 194, [P, RH])
    s_ps = [ctx.enter_context(nc.psum_tensor(f"r_s{i}", [P, HALF], F32)) for i in range(4)]
    t_ps = ctx.enter_context(nc.psum_tensor("r_t", [P, HALF], F32))
    g_ps = [ctx.enter_context(nc.psum_tensor(f"r_g{i}", [P, HALF], F32)) for i in range(2)]

    def sem(name):
        return ctx.enter_context(nc.semaphore("r_" + name))

    k_in, wq_in, wq_free, km_ready, km_copied = (sem("k_in"), [sem("wq_in0"), sem("wq_in1")], sem("wq_free"),
                                                 sem("km_ready"), sem("km_copied"))
    table, staged, scored, s_copied = sem("table"), sem("staged"), sem("scored"), sem("s_copied")
    step, exp_in, exp_out, rcg_ready, rcg_turned, rcg_copied = (
        sem("step"), sem("exp_in"), sem("exp_out"), sem("rcg_ready"), sem("rcg_turned"), sem("rcg_copied"))
    passed, cols_gated = sem("passed"), sem("cols_gated")
    hot_ready, g_ready, g_copied, g_out, g_free = (
        sem("hot_ready"), sem("g_ready"), sem("g_copied"), sem("g_out"), sem("g_free"))
    block = ctx.enter_context(nc.Block())
    GROUPS = P // GT
    GB = TB // GT

    def tiles(eng, body):
        with eng.Fori(0, TT - 1) as n:
            body(n, True)
        body(TT - 1, False)

    def blocks(eng, n, body):
        with eng.Fori(0, NB // 2) as i:
            for u in range(2):
                body(NB * n + 2 * i + u, u, 2 * i + u)

    @block.sync
    def _(sp):
        sp.dma_start(kT[:], keysT).then_inc(k_in, 16)
        for hp in range(2):
            sp.dma_start(wq[:, hp], wqT[hp]).then_inc(wq_in[hp], 16)
        with sp.Fori(1, HP // 2) as i:
            for u in range(2):
                sp.wait_ge(km_ready, 2 * (2 * i + u) - 2)
                sp.dma_start(wq[:, u], wqT[2 * i + u]).then_inc(wq_in[u], 16)

        def tile(n, more):
            def one(b, u, k):
                sp.wait_ge(g_copied, 2 + GB * (b + 1))
                sp.dma_start(g_scr[:, b], gblock[:, u]).then_inc(g_out, 16)
                sp.wait_ge(g_out, 16 * (b + 1))
                sp.sem_inc(g_free, 1)

            blocks(sp, n, one)

        tiles(sp, tile)

    @block.gpsimd
    def _(pool):
        nc.gpsimd.iota(iota_i[:], [[1, P]], base=0, channel_multiplier=0).then_inc(table, 1)
        pool.wait_ge(table, 1)
        nc.gpsimd.tensor_copy(iota[:], iota_i[:]).then_inc(table, 1)

    @block.scalar
    def _(act):
        act.sem_inc(km_copied, 4)
        act.sem_inc(g_copied, 2)
        act.sem_inc(g_free, 2)
        with act.Fori(0, HP // 2) as i:
            for u in range(2):
                for half in range(2):
                    act.wait_ge(km_ready, 2 * (2 * i + u) + half + 1)
                    nc.scalar.activation(km[:, 4 * half:4 * half + 4, bass.ds((2 * i + u) * NK, NK)],
                                         s_ps[2 * u + half][:].rearrange("p (c n) -> p c n", c=4),
                                         ACT.Copy).then_inc(km_copied, 1)

        def stage(n):
            nc.scalar.activation(ytile[:], yT[:, :, bass.ds(n * P, P)], ACT.Copy).then_inc(staged, 1)

        def copy_scores(n):
            for b in range(4):
                act.wait_ge(scored, 4 * n + b + 1)
                nc.scalar.activation(s[:, 4 * b:4 * b + 4, :], s_ps[b][:].rearrange("p (h n) -> p h n", h=4),
                                     ACT.Copy).then_inc(s_copied, 1)

        stage(0)
        copy_scores(0)

        def tile(n, more):
            if more:
                act.wait_ge(scored, 4 * n + 4)
                stage(n + 1)
            act.wait_ge(exp_in, n + 1)
            nc.scalar.activation(rcg[:, 2], rcg[:, 2], ACT.Exp).then_inc(exp_out, 1)
            act.wait_ge(rcg_turned, n + 1)
            nc.scalar.activation(rcgT[:], t_ps[:, 0:3 * P].rearrange("p (k t) -> p k t", k=3),
                                 ACT.Copy).then_inc(rcg_copied, 1)
            if more:
                copy_scores(n + 1)

            def gates_on(b, k, g):
                act.wait_ge(hot_ready, GB * b + g + 1)
                for t in range(GT):
                    ins = nc.scalar.activation(cols[:, g % HS, t], cols[:, g % HS, t], ACT.Copy,
                                               scale=rcgT[:, 2, bass.ds(k * TB + GT * g + t, 1)])
                ins.then_inc(cols_gated, 1)

            def one(b, u, k):
                act.wait_ge(g_free, b + 1)
                gates_on(b, k, 1)
                for g in range(GB):
                    if g % 2 and g + 2 < GB:
                        gates_on(b, k, g + 2)
                    act.wait_ge(g_ready, HS + GB * b + g + 1)
                    nc.scalar.activation(gblock[:, u, :, GT * g:GT * (g + 1)],
                                         g_ps[g % 2][:].rearrange("p (t j) -> p j t", t=GT),
                                         ACT.Copy).then_inc(g_copied, 1)

            blocks(act, n, one)

        tiles(act, tile)

    @block.vector
    def _(dve):
        dve.wait_ge(table, 2)
        i16 = iota[:, 0:TOPK].unsqueeze(1).unsqueeze(1).to_broadcast([P, RH, TOPK, TOPK])
        spread = lambda half, tok: rcgT[:, half, bass.ds(tok, GT)].unsqueeze(2).to_broadcast([P, GT, P])
        i128 = iota[:].unsqueeze(1).to_broadcast([P, GT, P])
        PER = 17

        def tile(n, more):
            count = [0]

            def seal(ins):
                ins.then_inc(step, 1)
                count[0] += 1
                dve.wait_ge(step, PER * n + count[0])
                dve.sem_inc(passed, 1)

            def top16(n_rows, values, spare, val, idx):
                for r in range(n_rows):
                    ins = nc.vector.max(val(r)[:, 0:8], values(r))
                seal(ins)
                for r in range(n_rows):
                    nc.vector.max_index(idx(r)[:, 0:8], val(r)[:, 0:8], values(r))
                for r in range(n_rows):
                    ins = nc.vector.match_replace(spare(r), val(r)[:, 0:8], values(r), NEG)
                seal(ins)
                for r in range(n_rows):
                    ins = nc.vector.max(val(r)[:, 8:16], spare(r))
                seal(ins)
                for r in range(n_rows):
                    ins = nc.vector.max_index(idx(r)[:, 8:16], val(r)[:, 8:16], spare(r))
                seal(ins)

            dve.wait_ge(s_copied, 4 * n + 4)
            dve.sem_inc(passed, 1)
            top16(HP, lambda r: s[:, r], lambda r: s2[:, r], lambda r: top[:, r // 2, r % 2, :], lambda r: topi[:, r])
            seal(nc.vector.tensor_tensor(cand[:].rearrange("p h (a b) -> p h a b", a=TOPK),
                                         top[:, :, 0, :].unsqueeze(3).to_broadcast([P, RH, TOPK, TOPK]),
                                         top[:, :, 1, :].unsqueeze(2).to_broadcast([P, RH, TOPK, TOPK]), ALU.add))
            top16(RH, lambda r: cand[:, r], lambda r: cand2[:, r], lambda r: best[:, r], lambda r: besti[:, r])
            gate = rcg[:, 2].rearrange("p (h e) -> p h e", h=RH)
            nc.vector.tensor_tensor(gate, best[:], best[:, :, 0:1].to_broadcast([P, RH, TOPK]),
                                    ALU.subtract).then_inc(exp_in, 1)
            nc.vector.tensor_scalar(ab[:, 0], besti[:], 4, None, ALU.logical_shift_right)
            nc.vector.tensor_scalar(ab[:, 1], besti[:], TOPK - 1, None, ALU.bitwise_and)
            seal(nc.vector.tensor_copy(topf[:], topi[:].rearrange("p (h a) k -> p h a k", a=2)))
            seal(nc.vector.tensor_copy(abf[:], ab[:]))
            for half in range(2):
                seal(nc.vector.tensor_tensor(hot[:], abf[:, half].unsqueeze(3).to_broadcast([P, RH, TOPK, TOPK]), i16,
                                             ALU.is_equal))
                seal(nc.vector.tensor_tensor(hot[:], hot[:],
                                             topf[:, :, half].unsqueeze(2).to_broadcast([P, RH, TOPK, TOPK]),
                                             ALU.mult))
                nc.vector.tensor_reduce(rcg[:, half].rearrange("p (h e) -> p h e", h=RH), hot[:], AX.X,
                                        ALU.add).then_inc(rcg_ready, 1)
                dve.wait_ge(rcg_ready, 3 * n + half + 1)
            dve.wait_ge(exp_out, n + 1)
            seal(nc.vector.tensor_reduce(esum[:], gate, AX.X, ALU.add))
            seal(nc.vector.reciprocal(esum[:], esum[:]))
            assert count[0] == PER
            nc.vector.tensor_tensor(gate, gate, esum[:].unsqueeze(2).to_broadcast([P, RH, TOPK]),
                                    ALU.mult).then_inc(rcg_ready, 1)
            dve.wait_ge(rcg_copied, n + 1)
            dve.sem_inc(passed, 1)

            def one(b, u, k):
                for g in range(GB):
                    dve.wait_ge(g_ready, GB * b + g + 1)
                    tok = k * TB + GT * g
                    nc.vector.tensor_tensor(rows[:, g % HS], i128, spread(0, tok), ALU.is_equal)
                    if g % 2:
                        ins = nc.vector.tensor_tensor(cols[:, g % HS], i128, spread(1, tok), ALU.is_equal)
                    else:
                        for t in range(GT):
                            ins = nc.vector.tensor_scalar(cols[:, g % HS, t], iota[:], rcgT[:, 1, bass.ds(tok + t, 1)],
                                                          rcgT[:, 2, bass.ds(tok + t, 1)], ALU.is_equal, ALU.mult)
                    ins.then_inc(hot_ready, 1)

            blocks(dve, n, one)

        tiles(dve, tile)

    @block.tensor
    def _(pe):
        pe.sem_inc(g_ready, HS)
        pe.wait_ge(k_in, 16)
        with pe.Fori(0, HP // 2) as i:
            for u in range(2):
                hp = 2 * i + u
                pe.wait_ge(wq_in[u], 16 * (i + 1))
                for half in range(2):
                    pe.wait_ge(km_copied, 2 * hp + half + 1)
                    for b in range(4):
                        c = 4 * half + b
                        ins = nc.tensor.matmul(s_ps[2 * u + half][:, b * NK:(b + 1) * NK], wq[:, u, c * P:(c + 1) * P],
                                               kT[:, hp, :], start=True, stop=True)
                    ins.then_inc(km_ready, 1)
        pe.wait_ge(km_copied, 4 + 2 * HP)

        def scores(n):
            pe.wait_ge(staged, n + 1)
            for b in range(4):
                for c in range(DC):
                    ins = nc.tensor.matmul(s_ps[b][:], ytile[:, c], km[:, c, b * HALF:(b + 1) * HALF], start=c == 0,
                                           stop=c == DC - 1)
                ins.then_inc(scored, 1)

        scores(0)

        def tile(n, more):
            if more:
                pe.wait_ge(s_copied, 4 * n + 4)
                scores(n + 1)
            pe.wait_ge(rcg_ready, 3 * n + 3)
            for k in range(3):
                ins = nc.tensor.transpose(t_ps[:, k * P:(k + 1) * P], rcg[:, k], ident[:])
            ins.then_inc(rcg_turned, 1)

            def one(b, u, k):
                for g in range(GB):
                    pe.wait_ge(hot_ready, GB * b + g + 1)
                    if g % 2:
                        pe.wait_ge(cols_gated, GB // 2 * b + g // 2 + 1)
                    pe.wait_ge(g_copied, GB * b + g + 1)
                    for t in range(GT):
                        ins = nc.tensor.matmul(g_ps[g % 2][:, t * P:(t + 1) * P], rows[:, g % HS, t], cols[:, g % HS, t],
                                               start=True, stop=True)
                    ins.then_inc(g_ready, 1)

            blocks(pe, n, one)

        tiles(pe, tile)


JG = 2
NGRP = NK // JG


def build_experts(nc, ctx, uT, v, yT, g_scr, acc):
    at = Place(nc)
    yh = [at("yT_hi", 0, [P, DC, T], F32R), at("yT_lo", 64, [P, DC, T], F32R)]
    A = [[at(f"A{r}{s}", 96 + 16 * r + 8 * s, [P, JG, T], F32R) for s in range(2)] for r in range(2)]
    u_raw = at("u_raw", 128, [P, JG, DC, P])
    uw = [at(f"u{s}", 136 + 8 * s, [P, JG, DC, P], F32R) for s in range(2)]
    v_raw = at("v_raw", 152, [P, JG, D])
    vw = [at(f"ve{s}", 160 + 8 * s, [P, JG, D], F32R) for s in range(2)]
    g_sb = at("g_sb", 176, [P, 2, T // TB, JG, TB])
    act_sb = at("act_sb", 192, [P, JG, T])
    s_ps = [ctx.enter_context(nc.psum_tensor(f"e_s{i}", [P, HALF], F32)) for i in range(2 * JG)]
    o_ps = [ctx.enter_context(nc.psum_tensor(f"e_o{i}", [P, HALF], F32)) for i in range(4)]

    def sem(name):
        return ctx.enter_context(nc.semaphore("e_" + name))

    y_hi, y_split, cleared = sem("y_hi"), sem("y_split"), sem("cleared")
    u_in, u_free, u_hi, u_split, u_done = sem("u_in"), sem("u_free"), sem("u_hi"), sem("u_split"), sem("u_done")
    v_in, v_free, v_hi, v_split, v_done = sem("v_in"), sem("v_free"), sem("v_hi"), sem("v_split"), sem("v_done")
    g_in, g_free = [sem("g_in0"), sem("g_in1")], sem("g_free")
    gelu, gated, A_hi, A_split, added = sem("gelu"), sem("gated"), sem("A_hi"), sem("A_split"), sem("added")
    block = ctx.enter_context(nc.Block())
    NU, NV = 2 * JG, 2 * TT

    def groups(eng, first, both, last):
        first()
        with eng.Fori(0, NGRP // 2 - 1) as i:
            both(2 * i, 0)
            both(2 * i + 1, 1)
        both(NGRP - 2, 0)
        last(NGRP - 1, 1)

    @block.sync
    def _(sp):
        def load_u(g):
            sp.wait_ge(u_free, g + 1)
            sp.dma_start(u_raw[:], uT[g]).then_inc(u_in, 16)

        def load_v(g):
            sp.wait_ge(v_free, g + 1)
            sp.dma_start(v_raw[:], v[:, g]).then_inc(v_in, 16)

        def load_g(g, r):
            sp.wait_ge(g_free, g + 1)
            sp.dma_start(g_sb[:, r].rearrange("p b j t -> p b (j t)"),
                         g_scr[:, :, bass.ds(g * JG, JG), :].rearrange("p b j t -> p b (j t)")).then_inc(g_in[r], 16)

        load_u(0)
        load_v(0)
        load_g(0, 0)
        load_u(1)
        load_g(1, 1)

        def both(g, r):
            load_v(g + 1)
            load_g(g + 2, r)
            load_u(g + 2)

        with sp.Fori(0, NGRP // 2 - 1) as i:
            both(2 * i, 0)
            both(2 * i + 1, 1)
        load_v(NGRP - 1)

    @block.scalar
    def _(act):
        def high_u(g):
            act.wait_ge(u_in, 16 * (g + 1))
            act.wait_ge(u_done, NU * g + NU)
            nc.scalar.activation(uw[0][:], u_raw[:], ACT.Copy).then_inc(u_hi, 1)

        def high_v(g):
            act.wait_ge(v_in, 16 * (g + 1))
            act.wait_ge(v_done, NV * g + NV)
            nc.scalar.activation(vw[0][:], v_raw[:], ACT.Copy).then_inc(v_hi, 1)

        def activate(g, r):
            for j in range(JG):
                for half in range(2):
                    act.wait_ge(u_done, NU + NU * g + 2 * j + half + 1)
                    act.wait_ge(A_split, JG * g + j + 1)
                    nc.scalar.activation(act_sb[:, j, half * HALF:(half + 1) * HALF], s_ps[2 * j + half][:],
                                         ACT.Gelu).then_inc(gelu, 1)
                if j:
                    high_a(g, r, j - 1)
            high_a(g, r, JG - 1)

        def high_a(g, r, j):
            act.wait_ge(gated, JG * g + j + 1)
            nc.scalar.activation(A[r][0][:, j], act_sb[:, j], ACT.Copy).then_inc(A_hi, 1)

        act.sem_inc(gelu, NU)

        def first():
            for c in range(DC):
                nc.scalar.activation(yh[0][:, c], yT[:, c], ACT.Copy).then_inc(y_hi, 1)
            high_u(0)
            activate(0, 0)
            high_u(1)

        def both(g, r):
            high_v(g)
            activate(g + 1, 1 - r)
            if not (isinstance(g, int) and g == NGRP - 2):
                high_u(g + 2)

        def last(g, r):
            high_v(g)

        groups(act, first, both, last)

    @block.vector
    def _(dve):
        dve.sem_inc(u_free, 1)
        dve.sem_inc(v_free, 1)
        dve.sem_inc(g_free, 2)
        dve.sem_inc(A_split, JG)

        def low_u(g):
            dve.wait_ge(u_hi, g + 1)
            nc.vector.tensor_tensor(uw[1][:], u_raw[:], uw[0][:].bitcast(F32), ALU.subtract).then_inc(u_split, 1)
            dve.wait_ge(u_split, g + 1)
            dve.sem_inc(u_free, 1)

        def low_v(g):
            dve.wait_ge(v_hi, g + 1)
            nc.vector.tensor_tensor(vw[1][:], v_raw[:], vw[0][:].bitcast(F32), ALU.subtract).then_inc(v_split, 1)
            dve.wait_ge(v_split, g + 1)
            dve.sem_inc(v_free, 1)

        def gate(g, r, k, between=nothing):
            dve.wait_ge(g_in[r], 16 * (k + 1))
            for j in range(JG):
                dve.wait_ge(gelu, NU + NU * g + 2 * j + 2)
                a = act_sb[:, j].rearrange("p (b t) -> p b t", t=TB)
                nc.vector.tensor_tensor(a, a, g_sb[:, r, :, j], ALU.mult).then_inc(gated, 1)
                if j:
                    low_a(g, r, j - 1)
            dve.wait_ge(gated, JG * g + JG)
            dve.sem_inc(g_free, 1)
            between(0, 2)
            low_a(g, r, JG - 1)

        def low_a(g, r, j):
            dve.wait_ge(A_hi, JG * g + j + 1)
            nc.vector.tensor_tensor(A[r][1][:, j], act_sb[:, j], A[r][0][:, j].bitcast(F32),
                                    ALU.subtract).then_inc(A_split, 1)

        def add(g, first=0, end=NV):
            for n in range(first, end):
                tt, half = n // 2, n % 2
                dve.wait_ge(v_done, NV + NV * g + n + 1)
                dve.wait_ge(added, NV * g + n + 1)
                sum_ = acc[:, tt, half * HALF:(half + 1) * HALF]
                nc.vector.tensor_tensor(sum_, sum_, o_ps[n % 4][:], ALU.add).then_inc(added, 1)

        def first():
            nc.vector.memset(acc[:], 0.0).then_inc(cleared, 1)
            dve.wait_ge(cleared, 1)
            dve.sem_inc(added, NV)
            for c in range(DC):
                dve.wait_ge(y_hi, c + 1)
                nc.vector.tensor_tensor(yh[1][:, c], yT[:, c], yh[0][:, c].bitcast(F32),
                                        ALU.subtract).then_inc(y_split, 1)
            low_u(0)
            gate(0, 0, 0)
            low_u(1)

        def both(g, r):
            low_v(g)
            k = half_of(g + 1)
            gate(g + 1, 1 - r, k, lambda first, end: add(g, first, end))
            add(g, 2, 4)
            if not (isinstance(g, int) and g == NGRP - 2):
                low_u(g + 2)
            add(g, 4)

        def last(g, r):
            low_v(g)
            add(g)

        first()
        with dve.Fori(0, NGRP // 2 - 1) as i:
            half_of = lambda g: i
            both(2 * i, 0)
            half_of = lambda g: i + 1
            both(2 * i + 1, 1)
        half_of = lambda g: NGRP // 2 - 1
        both(NGRP - 2, 0)
        last(NGRP - 1, 1)

    @block.tensor
    def _(pe):
        def u_products(g):
            pe.wait_ge(u_split, g + 1)
            for j in range(JG):
                for half in range(2):
                    pe.wait_ge(gelu, NU * g + 2 * j + half + 1)
                    split3(nc, s_ps[2 * j + half][:], uw, yh,
                           [(lambda t, c=c: t[:, j, c, :], lambda t, c=c: t[:, c, half * HALF:(half + 1) * HALF])
                            for c in range(DC)]).then_inc(u_done, 1)

        def v_products(g, r):
            pe.wait_ge(v_split, g + 1)
            pe.wait_ge(A_split, JG + JG * g + JG)
            for n in range(NV):
                tt, half = n // 2, n % 2
                pe.wait_ge(added, NV + NV * g + n - 3)
                split3(nc, o_ps[n % 4][:], A[r], vw,
                       [(lambda t, j=j: t[:, j, tt * P:(tt + 1) * P],
                         lambda t, j=j: t[:, j, half * HALF:(half + 1) * HALF])
                        for j in range(JG)]).then_inc(v_done, 1)

        def first():
            pe.sem_inc(u_done, NU)
            pe.sem_inc(v_done, NV)
            pe.wait_ge(y_split, DC)
            u_products(0)

        def both(g, r):
            u_products(g + 1)
            v_products(g, r)

        groups(pe, first, both, v_products)


def build_second_norm(nc, ctx, acc, y_scr, ln_g, ln_b, out):
    at = Place(nc)
    ys = at("ys", 96, [P, 2, D])
    z = at("z_e", 104, [P, D])
    yn = at("yn_e", 108, [P, 2, D])
    gb = at("gb_e", 116, [P, 2, D])
    st = at("st_e", 206.5, [P, 20])
    stats, mv, rstd, nmr, var, mhalf = (st[:, 0:12], st[:, 12:14], st[:, 14:15], st[:, 15:16], st[:, 16:17],
                                        st[:, 17:18])

    def sem(name):
        return ctx.enter_context(nc.semaphore("f_" + name))

    gb_in, const, y_in, z_ready, stat_step = sem("gb_in"), sem("const"), [sem("y_in0"), sem("y_in1")], sem(
        "z_ready"), sem("stat_step")
    rstd_ready, nmr_ready, yn_ready, scaled, ready, stored, passed, freed = (
        sem("rstd_ready"), sem("nmr_ready"), sem("yn_ready"), sem("scaled"), sem("ready"), sem("stored"),
        sem("passed"), sem("freed"))
    block = ctx.enter_context(nc.Block())

    def tiles(eng, body):
        with eng.Fori(0, TT // 2) as i:
            for u in range(2):
                body(2 * i + u, u, i)

    @block.sync
    def _(sp):
        sp.dma_start(gb[:, 0], ln_g.to_broadcast([P, D])).then_inc(gb_in, 16)
        sp.dma_start(gb[:, 1], ln_b.to_broadcast([P, D])).then_inc(gb_in, 16)

        def tile(n, u, i):
            sp.wait_ge(z_ready, n + 1)
            sp.dma_start(ys[:, u], y_scr[n]).then_inc(y_in[u], 16)

        tiles(sp, tile)

    @block.gpsimd
    def _(pool):
        nc.gpsimd.memset(mhalf, -0.5).then_inc(const, 1)
        pool.wait_ge(const, 1)

        def tile(n, u, i):
            pool.wait_ge(stat_step, 4 * n + 4)
            nc.gpsimd.tensor_tensor(rstd, var, mhalf, ALU.pow).then_inc(rstd_ready, 1)

        tiles(pool, tile)

    @block.scalar
    def _(act):
        act.sem_inc(yn_ready, 1)
        act.sem_inc(freed, 2)

        def tile(n, u, i):
            act.wait_ge(nmr_ready, n + 1)
            act.wait_ge(freed, n + 1)
            nc.scalar.activation(yn[:, u], z[:], ACT.Identity, scale=rstd, bias=nmr).then_inc(yn_ready, 1)
            act.wait_ge(ready, n + 1)
            act.dma_start(out[n], yn[:, u]).then_inc(stored, 16)
            act.wait_ge(stored, 16 * (n + 1))
            act.sem_inc(freed, 1)

        tiles(act, tile)

    @block.vector
    def _(dve):
        dve.sem_inc(z_ready, 2)
        dve.wait_ge(gb_in, 32)

        def tile(n, u, i):
            dve.wait_ge(y_in[u], 16 * (i + 1))
            dve.wait_ge(yn_ready, n + 1)
            nc.vector.scalar_tensor_tensor(z[:], ys[:, u], ALPHA, acc[:, n], ALU.mult, ALU.add).then_inc(z_ready, 1)
            dve.wait_ge(z_ready, n + 3)
            for half in range(2):
                nc.vector.bn_stats(stats[:, 6 * half:6 * half + 6],
                                   z[:, half * HALF:(half + 1) * HALF]).then_inc(stat_step, 1)
            dve.wait_ge(stat_step, 4 * n + 2)
            dve.sem_inc(passed, 1)
            nc.vector.bn_aggr(mv, stats).then_inc(stat_step, 1)
            dve.wait_ge(stat_step, 4 * n + 3)
            nc.vector.tensor_scalar(var, mv[:, 1:2], EPS, None, ALU.add).then_inc(stat_step, 1)
            dve.wait_ge(rstd_ready, n + 1)
            nc.vector.tensor_scalar(nmr, mv[:, 0:1], rstd, -1.0, ALU.mult, ALU.mult).then_inc(nmr_ready, 1)
            dve.wait_ge(yn_ready, n + 2)
            nc.vector.tensor_tensor(yn[:, u], yn[:, u], gb[:, 0], ALU.mult).then_inc(scaled, 1)
            dve.wait_ge(scaled, n + 1)
            nc.vector.tensor_tensor(yn[:, u], yn[:, u], gb[:, 1], ALU.add).then_inc(ready, 1)

        tiles(dve, tile)


def program(nc, a, out, debug):
    xT, w_in, subln = a["xT"], a["w_in"], a["subln"]
    lams = [a["lambda_" + n] for n in ("q1", "k1", "q2", "k2")]
    at = Place(nc)
    y_scr = nc.dram_tensor("y_scr", (TT, P, D), F32).ap()
    if debug not in ("A", "B"):
        g_scr = nc.dram_tensor("g_scr", (P, T // TB, NK, TB), F32).ap()
    xT_hi = at("xT_hi", 0, [P, DC, T], F32R)
    xT_lo = at("xT_lo", 32, [P, DC, T], F32R)
    oT = at("oT", 64, [P, H, T])
    ident = at("ident", 204, [P, P])
    with ExitStack() as ctx:
        build_attention(nc, ctx, xT, w_in, lams, subln, (ident, None), None, xT_hi, xT_lo, oT)
    if debug != "A":
        merged = at("merged", 96, [P, DC, T])
        with ExitStack() as ctx:
            build_branches(nc, ctx, w_in, a["pool_w"], a["pool_scale"], a["b_gate"], a["w_branch"], (xT_hi, xT_lo), oT,
                           merged)
    if debug not in ("A", "B"):
        yT = at("yT", 64, [P, DC, T])
        with ExitStack() as ctx:
            build_first_norm(nc, ctx, a["x"], a["w_out"], a["ln1_g"], a["ln1_b"], ident, merged, yT, y_scr)
        if debug != "C":
            with ExitStack() as ctx:
                build_retrieval(nc, ctx, a["wqT"], a["keysT"], ident, yT, g_scr)
    if debug == "":
        acc = at("acc", 32, [P, TT, D])
        with ExitStack() as ctx:
            build_experts(nc, ctx, a["uT"], a["v"], yT, g_scr, acc)
        with ExitStack() as ctx:
            build_second_norm(nc, ctx, acc, y_scr, a["ln2_g"], a["ln2_b"], out[0].rearrange("(n p) d -> n p d", p=P))
    if debug in ("C", "G"):
        merged = yT
    if debug in ("A", "B", "C", "G"):
        oT = oT if debug == "A" else merged
        with ExitStack() as ctx:
            st = ctx.enter_context(nc.semaphore("st"))
            block = ctx.enter_context(nc.Block())

            @block.sync
            def _(sp):
                sp.dma_start(out[0].rearrange("(h p) t -> p h t", p=P), oT[:]).then_inc(st, 16)
                sp.wait_ge(st, 16)


def kernel(**inputs):
    import concourse.bacc as bacc
    from concourse.bass_utils import run_bass_kernel_spmd

    one = {name: np.asarray(a)[0] for name, a in inputs.items()}
    blocks = one["w_in"].reshape(DC, P, -1, P).transpose(2, 1, 0, 3)
    arrays = {"xT": one["x"].T, "w_in": blocks, "subln": one["subln_g"][:, None]}
    arrays["x"] = one["x"].reshape(TT, P, D) if one["x"].ndim == 2 else one["x"]
    for n in ("ln1_g", "ln1_b", "ln2_g", "ln2_b"):
        arrays[n] = one[n][None, :]
    arrays["w_out"] = one["w_out"]
    arrays["uT"] = one["peer_u"].reshape(NK, NGRP, JG, DC, P).transpose(1, 4, 2, 3, 0)
    arrays["v"] = one["peer_v"].reshape(NK, NGRP, JG, D)
    arrays["wqT"] = one["peer_wq"].T.reshape(2 * RH, P, D)
    arrays["keysT"] = one["peer_subkeys"].reshape(2 * RH, NK, P).transpose(2, 0, 1)
    arrays["pool_w"] = one["pool_w"].transpose(1, 0, 2)
    arrays["pool_scale"] = one["pool_scale"].reshape(PG, P).T
    arrays["b_gate"] = one["b_gate"].reshape(2 * DC, P).T
    arrays["w_branch"] = np.concatenate([one["w_attn_proj"], one["w_pool_proj"]]).reshape(
        CA + CP, P, DC, P).transpose(2, 1, 0, 3)
    for n in ("lambda_q1", "lambda_k1", "lambda_q2", "lambda_k2"):
        arrays[n] = one[n][None, :]
    arrays = {k: np.ascontiguousarray(v) for k, v in arrays.items()}
    nc = bacc.Bacc("TRN2", target_bir_lowering=False, num_devices=1)
    aps = {k: nc.dram_tensor(k, v.shape, F32, kind="ExternalInput").ap() for k, v in arrays.items()}
    out = nc.dram_tensor("out", (1, T, D), F32, kind="ExternalOutput").ap()
    program(nc, aps, out, DEBUG)
    return run_bass_kernel_spmd(nc, [arrays], core_ids=[0]).results[0]["out"]


DEBUG = ""
```

```python
from contextlib import ExitStack

import numpy as np

import concourse.bass as bass
from concourse import mybir

F32 = mybir.dt.float32
F32R = mybir.dt.float32r
I32 = mybir.dt.int32
U32 = mybir.dt.uint32
ACT = mybir.ActivationFunctionType
ALU = mybir.AluOpType
AX = mybir.AxisListType

P = 128
T = 1024
D = 1024
TT = T // P
DC = D // P
HALF = 512
H = 8
DH = 64
DV = 128
PG = 4
WINDOWS = (2, 4, 8, 16)
RH = 8
NK = 128
TOPK = 16
ALPHA = 2.0 ** 0.25
EPS = 1e-5
LAM_INIT = 0.2
SCALE = DH ** -0.5
MASK = -1.0e30
KB = 1024


class Place:

    def __init__(self, nc):
        self.nc = nc

    def __call__(self, name, kib, shape, dtype=F32):
        return self.nc.alloc_sbuf_tensor_at(name, shape, dtype, offset=int(BASE + kib * KB))


BASE = 16512


def split3(nc, out, lhs, rhs, pairs, first=True, last=True, before=None):
    n = 0
    for i, (l, r) in enumerate(pairs):
        if before:
            before(i)
        for a, b in ((0, 0), (0, 1), (1, 0)):
            ins = nc.tensor.matmul(out, l(lhs[a]), r(rhs[b]), start=first and n == 0,
                                   stop=last and n == 3 * len(pairs) - 1)
            n += 1
    return ins


WQKV = 3
KEYS = [(qt + 1) * P for qt in range(TT)]
CHUNKS = [(k + HALF - 1) // HALF for k in KEYS]
S_USES = [(w, qt, c) for qt in range(TT) for w in range(2) for c in range(CHUNKS[qt])]
AT_USES = [(qt, c) for qt in range(TT) for c in range(CHUNKS[qt])]


def transpose_uses(first, more):
    uses = []
    for s in range(TT if more else TT + 3):
        if s - 3 >= (0 if first else -3):
            uses.append(("o", s - 3, 0))
        if s == TT - 1 and more:
            uses.append(("v", 0, 0))
        if s - 1 >= (0 if first else -1) and s <= TT:
            uses += [("a", s - 1, c) for c in range(CHUNKS[s - 1])]
    if more:
        uses.append(("v", 1, 0))
    return uses


NS, NA = len(S_USES), len(AT_USES)
INIT = 2


def tr_at(h, use, first, more, splits=False):
    keep = (lambda uses: [x for x in uses if not splits or x[0] != "o"])
    own, middle, opening = (keep(transpose_uses(*kind)) for kind in ((first, more), (False, True), (True, True)))
    shift = INIT + len(opening) - len(middle)
    if first:
        i = INIT + own.index(use)
        return i, i % 2
    if use in own:
        i = shift + own.index(use)
    else:
        i = shift - len(middle) + middle.index((use[0], use[1] + TT, use[2]))
    return len(middle) * h + i, i % 2


def locate(h, tile):
    return (h, tile) if tile >= 0 else (h - 1, tile + TT)


def build_attention(nc, ctx, passed, xT, w_in, lams, subln, const, oT_out, xT_hi, xT_lo, oT):
    at = Place(nc)
    x_raw = at("x_raw", 32, [P, DC, T])
    q = [[at(f"q{u}{s}", 96 + 16 * u + 4 * s, [P, T], F32R) for s in range(2)] for u in range(2)]
    k = [[at(f"k{u}{s}", 104 + 16 * u + 4 * s, [P, T], F32R) for s in range(2)] for u in range(2)]
    v = [[at(f"v{u}{s}", 128 + 8 * u + 4 * s, [P, TT, DV], F32R) for s in range(2)] for u in range(2)]
    w_raw = at("wa_raw", 144, [P, DC, P])
    w = [[at(f"wa{r}{s}", 148 + 8 * r + 4 * s, [P, DC, P], F32R) for s in range(2)] for r in range(2)]
    vT = at("vT", 164, [P, T])
    bias = at("bias", 168, [P, T])
    e = at("e", 172, [P, 2, T])
    a = [at("a0", 180, [P, T]), at("a1", 192, [P, T])]
    aT = [at(f"aT{s}", 184 + 4 * s, [P, 2, HALF], F32R) for s in range(2)]
    iota = at("iota_a", 192, [P, T], I32)
    ident, small = const
    osb = at("osb", 204 + 0.5, [P, DV])
    on = at("on", 204 + 1.0, [P, DV])
    sq = at("sq", 204 + 1.5, [P, DV])
    lam_in = at("lam_in", 196, [P, 4, DH])
    lam_t = at("lam_t", 197, [P, 2, DH])
    st = at("st_a", 204 + 2.0, [P, 32])
    mx, nmx, den, rden, ssq, rstd = (st[:, 0:4], st[:, 4:6], st[:, 6:8], st[:, 8:10], st[:, 10:11], st[:, 11:12])
    ms, mhalf, neglam, gain, le, lexp = (st[:, 12:13], st[:, 13:14], st[:, 14:15], st[:, 15:16], st[:, 16:18],
                                   st[:, 18:20])
    c2 = st[:, 20:21]

    s_ps = [ctx.enter_context(nc.psum_tensor(f"s_ps{i}", [P, HALF], F32)) for i in range(3)]
    j_ps = [ctx.enter_context(nc.psum_tensor(f"j_ps{i}", [P, HALF], F32)) for i in range(2)]
    t_ps = [ctx.enter_context(nc.psum_tensor(f"t_ps{i}", [P, HALF], F32)) for i in range(2)]
    o_ps = ctx.enter_context(nc.psum_tensor("o_ps", [P, DV], F32))

    def sem(name):
        return ctx.enter_context(nc.semaphore("a_" + name))

    x_in = [sem(f"x_in{c}") for c in range(DC)]
    x_hi, x_split = sem("x_hi"), sem("x_split")
    small_in, ready, tab = sem("small_in"), sem("consts_ready"), sem("table_steps")
    w_in_s, w_free, w_hi, w_split = (sem("w_in"), sem("w_raw_free"), sem("w_hi"), sem("w_split"))
    proj, qk_hi, qk_split, vT_copied, v_split = (sem("proj"), sem("qk_hi"), sem("qk_split"), sem("vT_copied"),
                                                 sem("v_split"))
    s_ready, s_free, mx_ready, e_ready, a_ready = (sem("s_ready"), sem("s_free"), sem("max_ready"), sem("e_ready"),
                                                   sem("a_ready"))
    tr_ready, tr_hi, tr_free = sem("tr_ready"), sem("tr_hi"), sem("tr_free")
    at_split, at_free = sem("aT_split"), sem("aT_free")
    o_free, ssq_ready, rstd_ready, on_ready = (sem("o_free"), sem("ssq_ready"),
                                                        sem("rstd_ready"), sem("on_ready"))
    pool_step, dve_step, act_step, bias_ready = sem("pool_step"), sem("dve_step"), sem("act_step"), sem("bias_ready")

    block = ctx.enter_context(nc.Block())

    def heads(eng, body):
        body(0, 0, True, True)
        with eng.Fori(0, H // 2 - 1) as i:
            body(2 * i + 1, 1, False, True)
            body(2 * i + 2, 0, False, True)
        body(H - 1, 1, False, False)

    def steps_of(first, more):
        low = 0 if first else -TT
        for s in range(TT if more else TT + 3):
            yield s, *((s - d if s - d >= low and s - d < TT else None) for d in (3, 1, 2))

    @block.sync
    def _(sp):
        def load_x(c):
            sp.dma_start(x_raw[:, c], xT[c * P:(c + 1) * P, :]).then_inc(x_in[c], 16)

        def load(n, blk):
            sp.wait_ge(w_free, n + 1)
            sp.dma_start(w_raw[:], w_in[blk]).then_inc(w_in_s, 16)

        load(0, 0)
        for c in range(DC):
            load_x(c)
        for r in range(1, WQKV):
            load(r, r * H)
        with sp.Fori(1, H) as h:
            for r in range(WQKV):
                load(WQKV * h + r, r * H + h)

    @block.gpsimd
    def _(pool):
        pool.sem_inc(w_free, 1)

        def split_weight(n, slot, wait):
            if wait:
                pool.wait_ge(proj, 2 * (n - 1))
            pool.wait_ge(w_in_s, 16 * (n + 1))
            pool.sem_inc(passed, 1)
            nc.gpsimd.tensor_copy(w[slot][0][:], w_raw[:]).then_inc(w_hi, 1)
            pool.wait_ge(w_hi, n + 1)
            nc.gpsimd.tensor_tensor(w[slot][1][:], w_raw[:], w[slot][0][:].bitcast(F32),
                                    ALU.subtract).then_inc(w_split, 1)
            pool.wait_ge(w_split, n + 1)
            pool.sem_inc(w_free, 1)

        split_weight(0, 0, False)
        nc.gpsimd.memset(ident[:], 0.0).then_inc(tab, 1)
        nc.gpsimd.iota(iota[:], [[1, T]], base=-(TT - 1) * P, channel_multiplier=-1).then_inc(tab, 1)
        nc.gpsimd.memset(mhalf, -0.5).then_inc(tab, 1)
        pool.wait_ge(tab, 3)
        nc.gpsimd.affine_select(out=ident[:], in_=ident[:], compare_op=ALU.not_equal, fill=1.0, base=0,
                                pattern=[[-1, P]], channel_multiplier=1).then_inc(tab, 1)
        nc.gpsimd.tensor_copy(bias[:], iota[:]).then_inc(tab, 1)
        pool.wait_ge(tab, 5)
        nc.gpsimd.affine_select(out=bias[:], in_=bias[:], compare_op=ALU.is_ge, fill=MASK, base=(TT - 1) * P,
                                pattern=[[-1, T]], channel_multiplier=1).then_inc(ready, 1)
        for r in range(1, WQKV):
            split_weight(r, r % 2, r >= 2)

        def head(h, u, first, more):
            for s, _, _, product in steps_of(first, more):
                if more and s in (0, 1, 3):
                    r = (0, 1, 3).index(s)
                    split_weight(WQKV * (h + 1) + r, (WQKV * (u + 1) + r) % 2, True)
                if product is not None:
                    m = TT * h + product
                    pool.wait_ge(ssq_ready, m + 1)
                    pool.sem_inc(passed, 1)
                    nc.gpsimd.tensor_scalar(ms, ssq, 1.0 / DV, EPS, ALU.mult, ALU.add).then_inc(pool_step, 1)
                    pool.wait_ge(pool_step, m + 1)
                    nc.gpsimd.tensor_tensor(rstd, ms, mhalf, ALU.pow).then_inc(rstd_ready, 1)

        heads(pool, head)

    @block.scalar
    def _(act):
        for i, l in enumerate(lams):
            act.dma_start(lam_in[:, i, :], l.to_broadcast([P, DH])).then_inc(small_in, 16)
        act.dma_start(gain, subln).then_inc(small_in, 16)
        act.sem_inc(o_free, 1)
        act.sem_inc(at_free, 2)
        for c in range(DC):
            act.wait_ge(x_in[c], 16)
            nc.scalar.activation(xT_hi[:, c], x_raw[:, c], ACT.Copy).then_inc(x_hi, 1)
        act.wait_ge(dve_step, 2)
        nc.scalar.activation(lexp, le, ACT.Exp).then_inc(act_step, 1)

        def evac(h, j, u):
            act.wait_ge(proj, 6 * h + j + 1)
            if j < 4:
                dst = (q, q, k, k)[j][u][0]
                nc.scalar.activation(dst[:, (j % 2) * HALF:(j % 2 + 1) * HALF], j_ps[j % 2][:],
                                     ACT.Copy).then_inc(qk_hi, 1)
            else:
                nc.scalar.activation(vT[:, (j % 2) * HALF:(j % 2 + 1) * HALF], j_ps[j % 2][:],
                                     ACT.Copy).then_inc(vT_copied, 1)


        for j in range(6):
            evac(0, j, 0)
        for half in range(2):
            act.wait_ge(tr_ready, half + 1)
            nc.scalar.activation(v[0][0][:, 4 * half:4 * half + 4, :],
                                 t_ps[half][:].rearrange("p (t d) -> p t d", t=4), ACT.Copy).then_inc(tr_hi, 1)

        def head(h, u, first, more):
            def tr_split(use):
                i, bank = tr_at(h, use, first, more)
                act.wait_ge(tr_ready, i + 1)
                if use[0] == "v":
                    dst = v[1 - u][0][:, 4 * use[1]:4 * use[1] + 4, :]
                    nc.scalar.activation(dst, t_ps[bank][:].rearrange("p (t d) -> p t d", t=4),
                                         ACT.Copy).then_inc(tr_hi, 1)
                    return
                hh, qt = locate(h, use[1])
                i_a = AT_USES.index((qt, use[2]))
                n = min(HALF, KEYS[qt] - use[2] * HALF)
                act.wait_ge(at_free, NA * hh + i_a + 1)
                nc.scalar.activation(aT[0][:, i_a % 2, 0:n], t_ps[bank][:, 0:n], ACT.Copy).then_inc(tr_hi, 1)

            def take_output(tile):
                hh, qt = locate(h, tile)
                m = TT * hh + qt
                act.wait_ge(at_free, 2 + NA * hh + AT_USES.index((qt, CHUNKS[qt] - 1)) + 1)
                if not (first and tile == 0):
                    act.wait_ge(on_ready, m)
                nc.scalar.activation(osb[:], o_ps[:], ACT.Copy).then_inc(o_free, 1)
                act.wait_ge(o_free, m + 2)
                nc.scalar.activation(sq[:], osb[:], ACT.Square, accum_out=ssq).then_inc(ssq_ready, 1)

            def scale_output(tile):
                act.wait_ge(rstd_ready, TT * h + tile + 1)
                if not (first and tile == 0):
                    act.wait_ge(tr_ready, tr_at(h, ("o", tile - 1, 0), first, more)[0] + 1)
                nc.scalar.activation(on[:], osb[:], ACT.Copy, scale=rstd).then_inc(on_ready, 1)

            for s, turned, transposed, product in steps_of(first, more):
                if s < TT:
                    act.wait_ge(mx_ready, TT * h + s + 1)
                    for wh in range(2):
                        nc.scalar.activation(e[:, wh, 0:KEYS[s]], e[:, wh, 0:KEYS[s]], ACT.Exp,
                                             bias=nmx[:, wh:wh + 1], accum_out=den[:, wh:wh + 1]).then_inc(e_ready, 1)
                if turned is not None:
                    scale_output(turned)
                if more and 1 <= s < 7:
                    evac(h + 1, s - 1, 1 - u)
                if product is not None:
                    take_output(product)
                if more and s == TT - 1:
                    tr_split(("v", 0, 0))
                if transposed is not None:
                    for c in range(CHUNKS[transposed]):
                        tr_split(("a", transposed, c))
            if more:
                tr_split(("v", 1, 0))

        heads(act, head)

    @block.vector
    def _(dve):
        steps = [0]

        def then(ins):
            steps[0] += 1
            ins.then_inc(dve_step, 1)
            dve.wait_ge(dve_step, steps[0])

        dve.sem_inc(s_free, 3)
        dve.sem_inc(tr_free, 2)
        dve.sem_inc(a_ready, 1)
        dve.wait_ge(small_in, 16 * 5)
        for i in range(2):
            then(nc.vector.tensor_tensor_reduce(lam_t[:, i, :], lam_in[:, 2 * i, :], lam_in[:, 2 * i + 1, :], 1.0, 0.0,
                                                ALU.mult, ALU.add, le[:, i:i + 1]))
        then(nc.vector.tensor_scalar(gain, gain, 1.0 - LAM_INIT, None, ALU.mult))
        for c in range(DC):
            dve.wait_ge(x_hi, c + 1)
            nc.vector.tensor_tensor(xT_lo[:, c], x_raw[:, c], xT_hi[:, c].bitcast(F32), ALU.subtract)\
                .then_inc(x_split, 1)
        dve.wait_ge(act_step, 1)
        then(nc.vector.tensor_tensor(neglam, lexp[:, 1:2], lexp[:, 0:1], ALU.subtract))
        then(nc.vector.tensor_scalar(neglam, neglam, -LAM_INIT, None, ALU.add))
        dve.wait_ge(ready, 1)
        then(nc.vector.tensor_scalar(bias[:], bias[:], 1.0 / SCALE, None, ALU.mult))
        setup = steps[0]

        def low(h, j, u):
            dve.wait_ge(qk_hi, 4 * h + j + 1)
            dst = (q, q, k, k)[j][u]
            half = slice((j % 2) * HALF, (j % 2 + 1) * HALF)
            nc.vector.tensor_tensor(dst[1][:, half], j_ps[j % 2][:], dst[0][:, half].bitcast(F32),
                                    ALU.subtract).then_inc(qk_split, 1)

        for j in range(4):
            low(0, j, 0)
        for half in range(2):
            dve.wait_ge(tr_hi, half + 1)
            part = slice(4 * half, 4 * half + 4)
            nc.vector.tensor_tensor(v[0][1][:, part, :], t_ps[half][:].rearrange("p (t d) -> p t d", t=4),
                                    v[0][0][:, part, :].bitcast(F32), ALU.subtract).then_inc(tr_free, 1)

        SM = 3
        HM = TT * SM + 1

        def head(h, u, first, more):
            def tr_low(use):
                i, bank = tr_at(h, use, first, more)
                ps = t_ps[bank]
                if use[0] == "o":
                    hh, qt = locate(h, use[1])
                    dve.wait_ge(tr_ready, i + 1)
                    nc.vector.tensor_scalar(oT[:, hh, qt * P:(qt + 1) * P], ps[:, 0:P], gain, None,
                                            ALU.mult).then_inc(tr_free, 1)
                    return
                dve.wait_ge(tr_hi, tr_at(h, use, first, more, True)[0] + 1)
                if use[0] == "v":
                    part = slice(4 * use[1], 4 * use[1] + 4)
                    nc.vector.tensor_tensor(v[1 - u][1][:, part, :], ps[:].rearrange("p (t d) -> p t d", t=4),
                                            v[1 - u][0][:, part, :].bitcast(F32), ALU.subtract).then_inc(tr_free, 1)
                    return
                qt = locate(h, use[1])[1]
                i_a = AT_USES.index((qt, use[2]))
                n = min(HALF, KEYS[qt] - use[2] * HALF)
                nc.vector.tensor_tensor(aT[1][:, i_a % 2, 0:n], ps[:, 0:n], aT[0][:, i_a % 2, 0:n].bitcast(F32),
                                        ALU.subtract).then_inc(tr_free, 1)

            at_step = setup + HM * h
            nc.vector.tensor_scalar(bias[:], bias[:], 0.5, None, ALU.mult).then_inc(dve_step, 1)
            dve.wait_ge(dve_step, at_step + 1)
            def logits(qt):
                m = TT * h + qt
                dve.wait_ge(a_ready, m + 1)
                for wh in range(2):
                    for c in range(CHUNKS[qt]):
                        i = S_USES.index((wh, qt, c))
                        n = min(HALF, KEYS[qt] - c * HALF)
                        dve.wait_ge(s_ready, NS * h + i + 1)
                        dve.sem_inc(passed, 1)
                        start = c * HALF + (TT - 1 - qt) * P
                        nc.vector.tensor_tensor_reduce(e[:, wh, c * HALF:c * HALF + n], s_ps[i % 3][:, 0:n],
                                                       bias[:, start:start + n], SCALE, -3.0e38, ALU.add, ALU.max,
                                                       mx[:, 2 * wh + c:2 * wh + c + 1]).then_inc(s_free, 1)
                i = S_USES.index((1, qt, CHUNKS[qt] - 1))
                dve.wait_ge(s_free, 3 + NS * h + i + 1)
                nc.vector.tensor_reduce(nmx, mx.rearrange("p (w c) -> p w c", w=2)[:, :, 0:CHUNKS[qt]], AX.X, ALU.max,
                                        negate=True).then_inc(mx_ready, 1)

            def combine(qt):
                base = at_step + 1 + SM * qt
                dve.wait_ge(e_ready, 2 * (TT * h + qt) + 2)
                nc.vector.reciprocal(rden, den).then_inc(dve_step, 1)
                dve.wait_ge(dve_step, base + 1)
                nc.vector.tensor_scalar(c2, rden[:, 1:2], neglam, None, ALU.mult).then_inc(dve_step, 1)
                dve.wait_ge(dve_step, base + 2)
                n = KEYS[qt]
                nc.vector.tensor_scalar(e[:, 1, 0:n], e[:, 1, 0:n], c2, None, ALU.mult).then_inc(dve_step, 1)
                dve.wait_ge(dve_step, base + 3)
                nc.vector.scalar_tensor_tensor(a[qt % 2][:, 0:n], e[:, 0, 0:n], rden[:, 0:1], e[:, 1, 0:n],
                                               ALU.mult, ALU.add).then_inc(a_ready, 1)

            for s, turned, transposed, _ in steps_of(first, more):
                if s < TT:
                    logits(s)
                    combine(s)
                if more and 1 <= s < 5:
                    low(h + 1, s - 1, 1 - u)
                if turned is not None:
                    tr_low(("o", turned, 0))
                if more and s == TT - 1:
                    tr_low(("v", 0, 0))
                if transposed is not None:
                    for c in range(CHUNKS[transposed]):
                        tr_low(("a", transposed, c))
            if more:
                tr_low(("v", 1, 0))

        heads(dve, head)

    @block.tensor
    def _(pe):
        def project(h, j, u):
            r, half = j // 2, j % 2
            if half == 0:
                pe.wait_ge(w_split, WQKV * h + r + 1)
            if not (isinstance(h, int) and h == 0 and j < 2):
                if j < 2:
                    pe.wait_ge(vT_copied, 2 * h - 1 + j)
                else:
                    pe.wait_ge(qk_split, 4 * h + j - 1)
            slot = (WQKV * u + r) % 2
            ins = split3(nc, j_ps[half][:], w[slot], (xT_hi, xT_lo),
                         [(lambda t, c=c: t[:, c, :], lambda t, c=c: t[:, c, half * HALF:(half + 1) * HALF])
                          for c in range(DC)],
                         before=(lambda c: pe.wait_ge(x_split, c + 1)) if isinstance(h, int) and h + j == 0 else None)
            ins.then_inc(proj, 1)

        def v_transposes(h, half, bank):
            pe.wait_ge(vT_copied, 2 * h + half + 1)
            for b in range(4):
                t = 4 * half + b
                ins = nc.tensor.transpose(t_ps[bank][:, b * P:(b + 1) * P], vT[:, t * P:(t + 1) * P], ident[:])
            ins.then_inc(tr_ready, 1)

        for j in range(6):
            project(0, j, 0)
        pe.wait_ge(tab, 5)
        for half in range(2):
            pe.wait_ge(tr_free, half + 1)
            v_transposes(0, half, half)

        def head(h, u, first, more):
            def scores(qt):
                if qt == 0:
                    pe.wait_ge(qk_split, 4 * h + 4)
                for wh in range(2):
                    rows = slice(wh * DH, (wh + 1) * DH)
                    for c in range(CHUNKS[qt]):
                        i = S_USES.index((wh, qt, c))
                        n = min(HALF, KEYS[qt] - c * HALF)
                        pe.wait_ge(s_free, NS * h + i + 1)
                        split3(nc, s_ps[i % 3][:, 0:n], q[u], k[u],
                               [(lambda t: t[rows, qt * P:(qt + 1) * P], lambda t: t[rows, c * HALF:c * HALF + n])]
                               ).then_inc(s_ready, 1)

            def turn(use):
                i, bank = tr_at(h, use, first, more)
                pe.wait_ge(tr_free, i + 1)
                if use[0] == "v":
                    v_transposes(h + 1, use[1], bank)
                elif use[0] == "o":
                    pe.wait_ge(on_ready, TT * h + use[1] + 1)
                    nc.tensor.transpose(t_ps[bank][:, 0:P], on[:], ident[:]).then_inc(tr_ready, 1)
                else:
                    qt = locate(h, use[1])[1]
                    if use[2] == 0:
                        pe.wait_ge(a_ready, 1 + TT * h + use[1] + 1)
                    for b in range(min(4, qt + 1 - 4 * use[2])):
                        start = use[2] * HALF + b * P
                        ins = nc.tensor.transpose(t_ps[bank][:, b * P:(b + 1) * P], a[qt % 2][:, start:start + P],
                                                  ident[:])
                    ins.then_inc(tr_ready, 1)

            def values(tile):
                hh, qt = locate(h, tile)
                pe.wait_ge(o_free, TT * hh + qt + 1)
                for c in range(CHUNKS[qt]):
                    i_a = AT_USES.index((qt, c))
                    pe.wait_ge(tr_free, 2 + tr_at(h, ("a", tile, c), first, more)[0] + 1)
                    blocks = range(min(4, qt + 1 - 4 * c))
                    ins = split3(nc, o_ps[:], aT, v[u if tile >= 0 else 1 - u],
                                 [(lambda t, b=b: t[:, i_a % 2, b * P:(b + 1) * P],
                                   lambda t, b=b: t[:, 4 * c + b, :]) for b in blocks],
                                 first=c == 0, last=c == CHUNKS[qt] - 1)
                    ins.then_inc(at_free, 1)

            for s, turned, transposed, product in steps_of(first, more):
                if s < TT:
                    scores(s)
                if more and 1 <= s < 7:
                    project(h + 1, s - 1, 1 - u)
                if product is not None:
                    values(product)
                if turned is not None:
                    turn(("o", turned, 0))
                if more and s == TT - 1:
                    turn(("v", 0, 0))
                if transposed is not None:
                    for c in range(CHUNKS[transposed]):
                        turn(("a", transposed, c))
            if more:
                turn(("v", 1, 0))

        heads(pe, head)


CA, CP = H, PG
PAD = 16


def build_branches(nc, ctx, w_in, pool_w, pool_scale, b_gate, w_branch, xT, oT, merged):
    at = Place(nc)
    pad = [at(f"pad{i}", 96 + 5 * i, [P, PAD + T]) for i in range(3)]
    pooled = [at(f"pooled{s}", 111 + 4 * s, [P, T], F32R) for s in range(2)]
    pw_raw = at("pw_raw", 119, [P, PG, P])
    pw = [at(f"pw{s}", 121 + 2 * s, [P, PG, P], F32R) for s in range(2)]
    count = at("count", 125, [P, PAD])
    icount = at("icount", 125.25, [P, PAD], I32)
    gates = at("gates", 96, [P, 2 * DC, T])
    pm_all = at("pm", 160, [P, PG, T])
    pm = [at("pm_hi", 32, [P, PG, T], F32R), at("pm_lo", 160, [P, PG, T], F32R)]
    w_raw = at("wb_raw", 176, [P, DC, P])
    w = [[at(f"wb{r}{s}", 180 + 8 * r + 4 * s, [P, DC, P], F32R) for s in range(2)] for r in range(2)]
    wc_raw = at("wc_raw", 200, [P, CA + CP, P])
    wc = [[at(f"wc{r}{s}", 176 + 12 * r + 6 * s, [P, CA + CP, P], F32R) for s in range(2)] for r in range(2)]
    o = [at("oT_hi", 0, [P, H, T], F32R), at("oT_lo", 64, [P, H, T], F32R)]
    branch = at("branch", 54, [P, 2, HALF])
    bg = at("bg", 206.5, [P, 2 * DC])
    psc = at("psc", 206.75, [P, PG])
    ps = [ctx.enter_context(nc.psum_tensor(f"b_ps{i}", [P, HALF], F32)) for i in range(8)]

    def sem(name):
        return ctx.enter_context(nc.semaphore("b_" + name))

    small_in, table, pw_hi = sem("small_in"), sem("table"), sem("pw_hi")
    w_raw_in, w_free, w_hi, w_split, unit = (sem("w_raw_in"), sem("w_free"), sem("w_hi"), sem("w_split"),
                                             sem("projected"))
    p_copied, p_step, pooled_hi, pooled_split, pm_unit, pm_scaled = (
        sem("p_copied"), sem("p_step"), sem("pooled_hi"), sem("pooled_split"), sem("pm_unit"), sem("pm_scaled"))
    gate_done = sem("gate_done")
    c_raw_in, c_free, c_hi, c_split, c_unit = (sem("c_raw_in"), sem("c_free"), sem("c_hi"), sem("c_split"),
                                               sem("branches"))
    o_hi, o_split, gated = sem("o_hi"), sem("o_split"), sem("gated")
    block = ctx.enter_context(nc.Block())
    NP = PG
    NG = 2 * DC
    FIRST = WQKV * H

    @block.sync
    def _(sp):
        sp.dma_start(pw_raw[:], pool_w).then_inc(small_in, 16)
        sp.dma_start(bg[:], b_gate).then_inc(small_in, 16)
        sp.dma_start(psc[:], pool_scale).then_inc(small_in, 16)
        with sp.Fori(0, NP + NG) as n:
            sp.wait_ge(w_free, n + 1)
            sp.dma_start(w_raw[:], w_in[n + FIRST]).then_inc(w_raw_in, 16)
        with sp.Fori(0, DC) as n:
            sp.wait_ge(c_free, n + 1)
            sp.dma_start(wc_raw[:], w_branch[n]).then_inc(c_raw_in, 16)

    @block.gpsimd
    def _(pool):
        nc.gpsimd.iota(icount[:], [[1, PAD]], base=1, channel_multiplier=0).then_inc(table, 1)
        nc.gpsimd.memset(pad[0][:, 0:PAD], 0.0).then_inc(table, 1)
        nc.gpsimd.memset(pad[1][:, 0:PAD], 0.0).then_inc(table, 1)
        nc.gpsimd.memset(pad[2][:, 0:PAD], 0.0).then_inc(table, 1)
        pool.sem_inc(w_free, 1)
        pool.sem_inc(c_free, 1)

        def low(n, r):
            pool.wait_ge(w_hi, n + 1)
            nc.gpsimd.tensor_tensor(w[r][1][:], w_raw[:], w[r][0][:].bitcast(F32), ALU.subtract).then_inc(w_split, 1)
            pool.wait_ge(w_split, n + 1)
            pool.sem_inc(w_free, 1)

        with pool.Fori(0, (NP + NG) // 2) as i:
            low(2 * i, 0)
            low(2 * i + 1, 1)
        with pool.Fori(0, DC // 2) as i:
            for r in range(2):
                n = 2 * i + r
                pool.wait_ge(c_hi, n + 1)
                nc.gpsimd.tensor_tensor(wc[r][1][:], wc_raw[:], wc[r][0][:].bitcast(F32),
                                        ALU.subtract).then_inc(c_split, 1)
                pool.wait_ge(c_split, n + 1)
                pool.sem_inc(c_free, 1)

    @block.scalar
    def _(act):
        def high(n, r, wait):
            act.wait_ge(w_raw_in, 16 * (n + 1))
            if wait:
                act.wait_ge(unit, 2 * (n - 1))
            nc.scalar.activation(w[r][0][:], w_raw[:], ACT.Copy).then_inc(w_hi, 1)

        act.sem_inc(gate_done, 4)
        act.wait_ge(small_in, 16 * 3)
        nc.scalar.activation(pw[0][:], pw_raw[:], ACT.Copy).then_inc(pw_hi, 1)
        high(0, 0, False)
        high(1, 1, False)
        for g in range(PG):
            for half in range(2):
                act.wait_ge(unit, 2 * g + half + 1)
                if g and not half:
                    act.wait_ge(p_step, 8 * g)
                nc.scalar.activation(pad[0][:, PAD + half * HALF:PAD + (half + 1) * HALF], ps[half][:],
                                     ACT.Copy).then_inc(p_copied, 1)
            high(g + 2, g % 2, True)
            act.wait_ge(p_step, 8 * (g + 1))
            if g:
                act.wait_ge(pm_unit, 2 * g)
            nc.scalar.activation(pooled[0][:], pad[1][:, PAD:], ACT.Copy).then_inc(pooled_hi, 1)
            for half in range(2):
                act.wait_ge(pm_unit, 2 * g + half + 1)
                nc.scalar.activation(pm_all[:, g, half * HALF:(half + 1) * HALF], ps[2 + half][:], ACT.Copy,
                                     scale=psc[:, g:g + 1]).then_inc(pm_scaled, 1)

        def gate(i, r):
            for half in range(2):
                act.wait_ge(unit, 2 * (i + NP) + half + 1)
                nc.scalar.activation(gates[:, i, half * HALF:(half + 1) * HALF], ps[4 + 2 * r + half][:], ACT.Sigmoid,
                                     bias=bg[:, bass.ds(i, 1)]).then_inc(gate_done, 1)

        with act.Fori(0, NG // 2 - 1) as i:
            for r in range(2):
                gate(2 * i + r, r)
                high(2 * i + r + NP + 2, r, True)
        gate(NG - 2, 0)
        gate(NG - 1, 1)
        def branch_high(n, r, wait):
            act.wait_ge(c_raw_in, 16 * (n + 1))
            if wait:
                act.wait_ge(c_unit, 4 * (n - 1))
            nc.scalar.activation(wc[r][0][:], wc_raw[:], ACT.Copy).then_inc(c_hi, 1)

        branch_high(0, 0, False)
        for c in range(H):
            nc.scalar.activation(o[0][:, c], oT[:, c], ACT.Copy).then_inc(o_hi, 1)
        for c in range(PG):
            nc.scalar.activation(pm[0][:, c], pm_all[:, c], ACT.Copy).then_inc(o_hi, 1)
        branch_high(1, 1, False)
        with act.Fori(1, DC // 2) as i:
            branch_high(2 * i, 0, True)
            branch_high(2 * i + 1, 1, True)

    @block.vector
    def _(dve):
        dve.wait_ge(table, 4)
        nc.vector.tensor_copy(count[:], icount[:]).then_inc(table, 1)
        dve.wait_ge(table, 5)
        nc.vector.reciprocal(count[:], count[:]).then_inc(table, 1)
        dve.wait_ge(table, 6)
        dve.wait_ge(pw_hi, 1)
        nc.vector.tensor_tensor(pw[1][:], pw_raw[:], pw[0][:].bitcast(F32), ALU.subtract).then_inc(pw_hi, 1)
        for g, window in enumerate(WINDOWS):
            step = 8 * g

            def then(ins, n):
                ins.then_inc(p_step, n)
                return n

            dve.wait_ge(p_copied, 2 * g + 2)
            if g:
                dve.wait_ge(pooled_hi, g)
            src = 0
            for level in range(g + 1):
                dst = 1 + (level + g + 1) % 2
                lag = 1 << level
                step += then(nc.vector.tensor_tensor(pad[dst][:, PAD:], pad[src][:, PAD:],
                                                     pad[src][:, PAD - lag:PAD + T - lag], ALU.add), 1)
                dve.wait_ge(p_step, step)
                src = dst
            dst = 3 - src
            step += then(nc.vector.tensor_tensor(pad[dst][:, PAD:PAD + window], pad[src][:, PAD:PAD + window],
                                                 count[:, 0:window], ALU.mult), 1)
            dve.wait_ge(p_step, step)
            step += then(nc.vector.tensor_tensor(pad[dst][:, PAD:PAD + window], pad[dst][:, PAD:PAD + window],
                                                 pad[0][:, PAD:PAD + window], ALU.subtract), 1)
            nc.vector.scalar_tensor_tensor(pad[dst][:, PAD + window:], pad[src][:, PAD + window:], 1.0 / window,
                                           pad[0][:, PAD + window:], ALU.mult,
                                           ALU.subtract).then_inc(p_step, 8 * (g + 1) - step)
            dve.wait_ge(pooled_hi, g + 1)
            nc.vector.tensor_tensor(pooled[1][:], pad[dst][:, PAD:], pooled[0][:].bitcast(F32),
                                    ALU.subtract).then_inc(pooled_split, 1)
            dve.wait_ge(pooled_split, g + 1)
        for c in range(H):
            dve.wait_ge(o_hi, c + 1)
            nc.vector.tensor_tensor(o[1][:, c], oT[:, c], o[0][:, c].bitcast(F32), ALU.subtract).then_inc(o_split, 1)
        for c in range(PG):
            dve.wait_ge(o_hi, H + c + 1)
            nc.vector.tensor_tensor(pm[1][:, c], pm_all[:, c], pm[0][:, c].bitcast(F32),
                                    ALU.subtract).then_inc(o_split, 1)
        dve.wait_ge(gate_done, 4 + 2 * NG)
        dve.sem_inc(gated, 12)
        with dve.Fori(0, DC // 2) as i:
            for r in range(2):
                n = 2 * i + r
                for half in range(2):
                    cols = slice(half * HALF, (half + 1) * HALF)
                    dve.wait_ge(c_unit, 4 * n + half + 1)
                    nc.vector.tensor_tensor(gates[:, n, cols], gates[:, n, cols], ps[4 * r + half][:],
                                            ALU.mult).then_inc(gated, 1)
                for half in range(2):
                    cols = slice(half * HALF, (half + 1) * HALF)
                    dve.wait_ge(c_unit, 4 * n + 2 + half + 1)
                    nc.vector.tensor_tensor(branch[:, half], gates[:, n + DC, cols], ps[4 * r + 2 + half][:],
                                            ALU.mult).then_inc(gated, 1)
                dve.wait_ge(gated, 12 + 6 * n + 4)
                for half in range(2):
                    cols = slice(half * HALF, (half + 1) * HALF)
                    nc.vector.tensor_tensor(merged[:, n, cols], gates[:, n, cols], branch[:, half],
                                            ALU.add).then_inc(gated, 1)
                dve.wait_ge(gated, 12 + 6 * n + 6)

    @block.tensor
    def _(pe):
        def product(out, lhs, rhs, half, chunks, before=None):
            return split3(nc, out, lhs, rhs,
                          [(lambda t, c=c: t[:, c[0], :], lambda t, c=c: t[:, c[1], half * HALF:(half + 1) * HALF])
                           for c in chunks], before=before)

        def pool_product(g):
            pe.wait_ge(pw_hi, 2)
            pe.wait_ge(pooled_split, g + 1)
            for half in range(2):
                if g:
                    pe.wait_ge(pm_scaled, 2 * g - 1 + half)
                split3(nc, ps[2 + half][:], pw, pooled,
                       [(lambda t: t[:, g, :], lambda t: t[:, half * HALF:(half + 1) * HALF])]).then_inc(pm_unit, 1)

        for g in range(PG):
            for half in range(2):
                if not half:
                    pe.wait_ge(w_split, g + 1)
                if g:
                    pe.wait_ge(p_copied, 2 * g - 1 + half)
                product(ps[half][:], w[g % 2], xT, half, [(c, c) for c in range(DC)]).then_inc(unit, 1)
            if g:
                pool_product(g - 1)
        pool_product(PG - 1)
        with pe.Fori(0, NG // 2) as i:
            for r in range(2):
                n = 2 * i + r
                pe.wait_ge(w_split, n + NP + 1)
                for half in range(2):
                    pe.wait_ge(gate_done, 2 * n + half + 1)
                    product(ps[4 + 2 * r + half][:], w[r], xT, half, [(c, c) for c in range(DC)]).then_inc(unit, 1)
        pe.wait_ge(gate_done, 4 + 2 * NG)
        with pe.Fori(0, DC // 2) as i:
            for r in range(2):
                n = 2 * i + r
                pe.wait_ge(c_split, n + 1)
                pe.wait_ge(gated, 6 * n + 4)
                for half in range(2):
                    product(ps[4 * r + half][:], wc[r], o, half, [(c, c) for c in range(CA)],
                            lambda c: pe.wait_ge(o_split, c + 1)).then_inc(c_unit, 1)
                for half in range(2):
                    product(ps[4 * r + 2 + half][:], wc[r], pm, half, [(CA + c, c) for c in range(CP)],
                            lambda c: pe.wait_ge(o_split, CA + c + 1)).then_inc(c_unit, 1)


def lagged(eng, front, back):
    front(0, 0)
    with eng.Fori(0, TT // 2 - 1) as i:
        for u in (1, 0):
            n = 2 * i + 2 - u
            front(n, u)
            back(n - 1, 1 - u)
    front(TT - 1, 1)
    back(TT - 2, 0)
    back(TT - 1, 1)


def nothing(n, u):
    pass


def build_first_norm(nc, ctx, passed, x, w_out, ln_g, ln_b, ident, merged, yT, y_scr):
    at = Place(nc)
    w_raw = at("wo_raw", 0, [P, DC, D])
    w = [at("wo_hi", 32, [P, DC, D], F32R), at("wo_lo", 0, [P, DC, D], F32R)]
    m = [[at(f"mt{u}{s}", 128 + 8 * u + 4 * s, [P, DC, P], F32R) for s in range(2)] for u in range(2)]
    xs = at("xs", 144, [P, 2, D])
    z = at("z", 152, [P, D])
    yn = at("yn", 156, [P, D])
    y = at("y", 160, [P, 2, D])
    gb = at("gb", 168, [P, 2, D])
    st = at("st_c", 206.5, [P, 20])
    stats, mv, rstd, nmr, var, mhalf = (st[:, 0:12], st[:, 12:14], st[:, 14:15], st[:, 15:16], st[:, 16:17],
                                        st[:, 17:18])
    mix = [[ctx.enter_context(nc.psum_tensor(f"mix{u}{h}", [P, HALF], F32)) for h in range(2)] for u in range(2)]
    t_ps = [ctx.enter_context(nc.psum_tensor(f"ct_ps{i}", [P, HALF], F32)) for i in range(2)]

    def sem(name):
        return ctx.enter_context(nc.semaphore("c_" + name))

    w_in_s = [sem(f"w_in{c}") for c in range(DC)]
    w_hi, w_split, gb_in, const = sem("w_hi"), sem("w_split"), sem("gb_in"), sem("const")
    x_in, m_hi, m_split, mixed, z_ready = sem("x_in"), sem("m_hi"), sem("m_split"), sem("mixed"), sem("z_ready")
    stat_step, rstd_ready, nmr_ready, yn_ready = sem("stat_step"), sem("rstd_ready"), sem("nmr_ready"), sem("yn_ready")
    y_scaled, y_ready, y_out, y_free = sem("y_scaled"), sem("y_ready"), sem("y_out"), sem("y_free")
    tr_ready, tr_copied = sem("tr_ready"), sem("tr_copied")
    block = ctx.enter_context(nc.Block())

    @block.sync
    def _(sp):
        for c in range(DC):
            sp.dma_start(w_raw[:, c], w_out[c * P:(c + 1) * P, :]).then_inc(w_in_s[c], 16)
        sp.dma_start(gb[:, 0], ln_g.to_broadcast([P, D])).then_inc(gb_in, 16)
        sp.dma_start(gb[:, 1], ln_b.to_broadcast([P, D])).then_inc(gb_in, 16)
        sp.sem_inc(y_free, 2)

        def front(n, u):
            sp.wait_ge(z_ready, 2 * n + 2)
            sp.dma_start(xs[:, u], x[n]).then_inc(x_in, 16)
            sp.wait_ge(x_in, 16 * (n + 1))

        def back(n, u):
            sp.wait_ge(y_ready, n + 1)
            sp.dma_start(y_scr[n], y[:, u]).then_inc(y_out, 16)
            sp.wait_ge(y_out, 16 * (n + 1))
            sp.sem_inc(y_free, 1)

        lagged(sp, front, back)

    @block.gpsimd
    def _(pool):
        nc.gpsimd.memset(mhalf, -0.5).then_inc(const, 1)
        pool.wait_ge(const, 1)

        def back(n, u):
            pool.wait_ge(stat_step, 4 * n + 4)
            nc.gpsimd.tensor_tensor(rstd, var, mhalf, ALU.pow).then_inc(rstd_ready, 1)

        lagged(pool, nothing, back)

    @block.scalar
    def _(act):
        act.sem_inc(yn_ready, 1)
        act.sem_inc(tr_copied, 2)

        def high_m(n, u):
            act.wait_ge(mixed, 2 * n + 2)
            nc.scalar.activation(m[u][0][:], merged[:, :, bass.ds(n * P, P)], ACT.Copy).then_inc(m_hi, 1)

        high_m(0, 0)
        for c in range(DC):
            act.wait_ge(w_in_s[c], 16)
            nc.scalar.activation(w[0][:, c], w_raw[:, c], ACT.Copy).then_inc(w_hi, 1)

        def front(n, u):
            if not (isinstance(n, int) and n == 0):
                high_m(n, u)

        def back(n, u):
            act.wait_ge(nmr_ready, n + 1)
            act.wait_ge(y_scaled, n + 1)
            nc.scalar.activation(yn[:], z[:], ACT.Identity, scale=rstd, bias=nmr).then_inc(yn_ready, 1)
            for half in range(2):
                act.wait_ge(tr_ready, 2 * n + half + 1)
                nc.scalar.activation(yT[:, 4 * half:4 * half + 4, bass.ds(n * P, P)],
                                     t_ps[half][:].rearrange("p (c t) -> p c t", c=4),
                                     ACT.Copy).then_inc(tr_copied, 1)

        lagged(act, front, back)

    @block.vector
    def _(dve):
        dve.sem_inc(z_ready, 4)
        dve.sem_inc(y_scaled, 1)

        def low_m(n, u):
            dve.wait_ge(m_hi, n + 1)
            nc.vector.tensor_tensor(m[u][1][:], merged[:, :, bass.ds(n * P, P)], m[u][0][:].bitcast(F32),
                                    ALU.subtract).then_inc(m_split, 1)

        low_m(0, 0)
        for c in range(DC):
            dve.wait_ge(w_hi, c + 1)
            nc.vector.tensor_tensor(w[1][:, c], w_raw[:, c], w[0][:, c].bitcast(F32),
                                    ALU.subtract).then_inc(w_split, 1)
        dve.wait_ge(gb_in, 32)

        def front(n, u):
            if not (isinstance(n, int) and n == 0):
                low_m(n, u)

        def back(n, u):
            dve.wait_ge(x_in, 16 * (n + 1))
            dve.wait_ge(yn_ready, n + 1)
            for half in range(2):
                cols = slice(half * HALF, (half + 1) * HALF)
                dve.wait_ge(mixed, 4 + 2 * n + half + 1)
                nc.vector.scalar_tensor_tensor(z[:, cols], xs[:, u, cols], ALPHA, mix[u][half][:], ALU.mult,
                                               ALU.add).then_inc(z_ready, 1)
            for half in range(2):
                dve.wait_ge(z_ready, 4 + 2 * n + half + 1)
                nc.vector.bn_stats(stats[:, 6 * half:6 * half + 6],
                                   z[:, half * HALF:(half + 1) * HALF]).then_inc(stat_step, 1)
            dve.wait_ge(stat_step, 4 * n + 2)
            dve.sem_inc(passed, 1)
            nc.vector.bn_aggr(mv, stats).then_inc(stat_step, 1)
            dve.wait_ge(stat_step, 4 * n + 3)
            nc.vector.tensor_scalar(var, mv[:, 1:2], EPS, None, ALU.add).then_inc(stat_step, 1)
            dve.wait_ge(rstd_ready, n + 1)
            nc.vector.tensor_scalar(nmr, mv[:, 0:1], rstd, -1.0, ALU.mult, ALU.mult).then_inc(nmr_ready, 1)
            dve.wait_ge(y_free, n + 1)
            dve.wait_ge(yn_ready, n + 2)
            nc.vector.tensor_tensor(y[:, u], yn[:], gb[:, 0], ALU.mult).then_inc(y_scaled, 1)
            dve.wait_ge(y_scaled, n + 2)
            nc.vector.tensor_tensor(y[:, u], y[:, u], gb[:, 1], ALU.add).then_inc(y_ready, 1)

        lagged(dve, front, back)

    @block.tensor
    def _(pe):
        pe.sem_inc(mixed, 4)

        def front(n, u):
            pe.wait_ge(m_split, n + 1)
            pe.wait_ge(z_ready, 2 * n + 2)
            for half in range(2):
                split3(nc, mix[u][half][:], m[u], w,
                       [(lambda t, c=c: t[:, c, :], lambda t, c=c: t[:, c, half * HALF:(half + 1) * HALF])
                        for c in range(DC)],
                       before=(lambda c: pe.wait_ge(w_split, c + 1)) if isinstance(n, int) and n + half == 0 else None
                       ).then_inc(mixed, 1)

        def back(n, u):
            pe.wait_ge(y_ready, n + 1)
            for half in range(2):
                pe.wait_ge(tr_copied, 2 * n + half + 1)
                for b in range(4):
                    c = 4 * half + b
                    ins = nc.tensor.transpose(t_ps[half][:, b * P:(b + 1) * P], y[:, u, c * P:(c + 1) * P], ident[:])
                ins.then_inc(tr_ready, 1)

        lagged(pe, front, back)


HP = 2 * RH
CAND = TOPK * TOPK
UC = 4
UU = 2 * UC
GE = 4
HS = 4
TB = 32
GT = 4
NB = P // TB
NEG = -3.0e38


def build_retrieval(nc, ctx, passed, wqT, keysT, uT, ident, yT, yh, g_scr, a_scr):
    at = Place(nc)
    km = at("km", 0, [P, DC, HP * NK])
    wq = at("wq", 128, [P, 2, D])
    kT = at("kT", 136, [P, HP, NK])
    gblock = at("gblock", 128, [P, 2, NK, TB])
    ytile = at("ytile", 160, [P, DC, P])
    s = at("s", 164, [P, HP, NK])
    cand2 = at("cand2", 164, [P, RH, CAND])
    topf = at("topf", 164, [P, RH, 2, TOPK])
    ab = at("ab", 165, [P, 2, RH, TOPK], U32)
    abf = at("abf", 166, [P, 2, RH, TOPK])
    s2 = at("s2", 172, [P, HP, NK])
    cand = at("cand", 172, [P, RH, CAND])
    hot = at("hot", 172, [P, RH, TOPK, TOPK])
    rows = at("rows", 172, [P, HS, GT, P])
    cols = at("cols", 180, [P, HS, GT, P])
    top = at("top", 188, [P, RH, 2, TOPK])
    topi = at("topi", 189, [P, HP, TOPK], U32)
    best = at("best", 190, [P, RH, TOPK])
    besti = at("besti", 190.5, [P, RH, TOPK], U32)
    iota_i = at("iota_i", 191, [P, P], I32)
    rcg = at("rcg", 191, [P, 3, P])
    rcgT = at("rcgT", 192.5, [P, 3, P])
    iota = at("iota_r", 194, [P, P])
    esum = at("esum", 194.5, [P, RH])
    uc_raw = at("uc_raw", 195, [P, DC, P])
    uc = [at("uc_hi", 199, [P, DC, P], F32R), at("uc_lo", 195, [P, DC, P], F32R)]
    act_col = at("act_col", 203, [P, T])
    s_ps = [ctx.enter_context(nc.psum_tensor(f"r_s{i}", [P, HALF], F32)) for i in range(4)]
    t_ps = ctx.enter_context(nc.psum_tensor("r_t", [P, HALF], F32))
    g_ps = [ctx.enter_context(nc.psum_tensor(f"r_g{i}", [P, HALF], F32)) for i in range(2)]
    u_ps = ctx.enter_context(nc.psum_tensor("r_u", [P, HALF], F32))

    def sem(name):
        return ctx.enter_context(nc.semaphore("r_" + name))

    k_in, wq_in, wq_free, km_ready, km_copied = (sem("k_in"), [sem("wq_in0"), sem("wq_in1")], sem("wq_free"),
                                                 sem("km_ready"), sem("km_copied"))
    table, staged, scored, s_copied = sem("table"), sem("staged"), sem("scored"), sem("s_copied")
    step, exp_in, exp_out, rcg_ready, rcg_turned, rcg_copied = (
        sem("step"), sem("exp_in"), sem("exp_out"), sem("rcg_ready"), sem("rcg_turned"), sem("rcg_copied"))
    cols_gated = sem("cols_gated")
    y_hi, y_split, u_in, u_hi, u_split = sem("y_hi"), sem("y_split"), sem("u_in"), sem("u_hi"), sem("u_split")
    unit_done, unit_free, act_out = sem("unit_done"), sem("unit_free"), sem("act_out")
    hot_ready, g_ready, g_copied, g_out, g_free = (
        sem("hot_ready"), sem("g_ready"), sem("g_copied"), sem("g_out"), sem("g_free"))
    block = ctx.enter_context(nc.Block())
    GROUPS = P // GT
    GB = TB // GT

    def tiles(eng, body):
        with eng.Fori(0, TT - 1) as n:
            body(n, True)
        body(TT - 1, False)

    def blocks(eng, n, body, pair=False):
        with eng.Fori(0, NB // 2) as i:
            for u in range(2):
                body(NB * n + 2 * i + u, u, 2 * i + u, *((i,) if pair else ()))

    @block.sync
    def _(sp):
        sp.dma_start(kT[:], keysT).then_inc(k_in, 16)
        for hp in range(2):
            sp.dma_start(wq[:, hp], wqT[hp]).then_inc(wq_in[hp], 16)
        with sp.Fori(1, HP // 2) as i:
            for u in range(2):
                sp.wait_ge(km_ready, 2 * (2 * i + u) - 2)
                sp.dma_start(wq[:, u], wqT[2 * i + u]).then_inc(wq_in[u], 16)

        def tile(n, more):
            def one(b, u, k):
                sp.wait_ge(g_copied, 2 + GB * (b + 1))
                sp.dma_start(g_scr[:, b], gblock[:, u]).then_inc(g_out, 16)
                sp.wait_ge(g_out, 16 * (b + 1))
                sp.sem_inc(g_free, 1)

            blocks(sp, n, one)

        tiles(sp, tile)

    @block.gpsimd
    def _(pool):
        nc.gpsimd.iota(iota_i[:], [[1, P]], base=0, channel_multiplier=0).then_inc(table, 1)
        pool.wait_ge(table, 1)
        nc.gpsimd.tensor_copy(iota[:], iota_i[:]).then_inc(table, 1)

        def tile(n, more):
            for k in range(UC):
                pool.wait_ge(u_in, 16 * (UC * n + k + 1))
                pool.sem_inc(passed, 1)
                nc.gpsimd.tensor_copy(uc[0][:], uc_raw[:]).then_inc(u_hi, 1)
                pool.wait_ge(u_hi, UC * n + k + 1)
                nc.gpsimd.tensor_tensor(uc[1][:], uc_raw[:], uc[0][:].bitcast(F32), ALU.subtract).then_inc(u_split, 1)

        tiles(pool, tile)

    @block.scalar
    def _(act):
        act.sem_inc(km_copied, 4)
        act.sem_inc(g_copied, 2)
        act.sem_inc(g_free, 2)
        act.sem_inc(unit_free, 1)
        act.dma_start(uc_raw[:], uT[0]).then_inc(u_in, 16)
        for c in range(DC):
            nc.scalar.activation(yh[0][:, c], yT[:, c], ACT.Copy).then_inc(y_hi, 1)
        with act.Fori(0, HP // 2) as i:
            for u in range(2):
                for half in range(2):
                    act.wait_ge(km_ready, 2 * (2 * i + u) + half + 1)
                    nc.scalar.activation(km[:, 4 * half:4 * half + 4, bass.ds((2 * i + u) * NK, NK)],
                                         s_ps[2 * u + half][:].rearrange("p (c n) -> p c n", c=4),
                                         ACT.Copy).then_inc(km_copied, 1)

        def copy_scores(n):
            for b in range(4):
                act.wait_ge(scored, 4 * n + b + 1)
                nc.scalar.activation(s[:, 4 * b:4 * b + 4, :], s_ps[b][:].rearrange("p (h n) -> p h n", h=4),
                                     ACT.Copy).then_inc(s_copied, 1)

        copy_scores(0)

        def activate(n, unit, half, col):
            act.wait_ge(unit_done, unit + 1)
            nc.scalar.activation(act_col[:, half * HALF:(half + 1) * HALF], u_ps[:], ACT.Gelu).then_inc(unit_free, 1)
            if half:
                act.wait_ge(unit_free, unit + 2)
                act.dma_start(a_scr[:, col], act_col[:]).then_inc(act_out, 16)

        def load_u(col):
            act.dma_start(uc_raw[:], uT[col]).then_inc(u_in, 16)

        def tile(n, more):
            for k in range(3):
                if k == 2:
                    act.wait_ge(act_out, 16 * (UC * n + 1))
                activate(n, UU * n + k, k % 2, UC * n + k // 2)
                if k == 1:
                    load_u(UC * n + 1)
            act.wait_ge(exp_in, n + 1)
            nc.scalar.activation(rcg[:, 2], rcg[:, 2], ACT.Exp).then_inc(exp_out, 1)
            act.wait_ge(rcg_turned, n + 1)
            nc.scalar.activation(rcgT[:], t_ps[:, 0:3 * P].rearrange("p (k t) -> p k t", k=3),
                                 ACT.Copy).then_inc(rcg_copied, 1)
            activate(n, UU * n + 3, 1, UC * n + 1)
            load_u(UC * n + 2)
            if more:
                copy_scores(n + 1)

            def gates_on(b, k, g):
                act.wait_ge(hot_ready, GB * b + g + 1)
                for t in range(GT):
                    ins = nc.scalar.activation(cols[:, g % HS, t], cols[:, g % HS, t], ACT.Copy,
                                               scale=rcgT[:, 2, bass.ds(k * TB + GT * g + t, 1)])
                ins.then_inc(cols_gated, 1)

            def one(b, u, k, i):
                act.wait_ge(g_free, b + 1)
                gates_on(b, k, 1)
                for g in range(GB):
                    if g == 2:
                        gates_on(b, k, 1 + GE)
                    act.wait_ge(g_ready, HS + GB * b + g + 1)
                    nc.scalar.activation(gblock[:, u, :, GT * g:GT * (g + 1)],
                                         g_ps[g % 2][:].rearrange("p (t j) -> p j t", t=GT),
                                         ACT.Copy).then_inc(g_copied, 1)
                    if u == 1 and g == GB // 2:
                        activate(n, UU * n + 4 + 2 * i + 1, 1, UC * n + 2 + i)
                        load_u(UC * n + 3 + i)
                if u == 0:
                    act.wait_ge(act_out, 16 * (UC * n + 2 + i))
                    activate(n, UU * n + 4 + 2 * i, 0, None)

            blocks(act, n, one, True)
            act.wait_ge(act_out, 16 * (UC * n + UC))
            if not more:
                act.wait_ge(u_in, 16 * (UC * TT + 1))
            act.sem_inc(passed, 1)

        tiles(act, tile)

    @block.vector
    def _(dve):
        for c in range(DC):
            dve.wait_ge(y_hi, c + 1)
            nc.vector.tensor_tensor(yh[1][:, c], yT[:, c], yh[0][:, c].bitcast(F32), ALU.subtract).then_inc(y_split, 1)
        dve.wait_ge(y_split, DC)

        def stage(n):
            part = [t[:, :, bass.ds(n * P, P)].bitcast(F32) for t in yh]
            nc.vector.tensor_tensor(ytile[:], part[0], part[1], ALU.add).then_inc(staged, 1)

        stage(0)
        dve.wait_ge(table, 2)
        i16 = iota[:, 0:TOPK].unsqueeze(1).unsqueeze(1).to_broadcast([P, RH, TOPK, TOPK])
        spread = lambda half, tok: rcgT[:, half, bass.ds(tok, GT)].unsqueeze(2).to_broadcast([P, GT, P])
        i128 = iota[:].unsqueeze(1).to_broadcast([P, GT, P])
        PER = 17

        def tile(n, more):
            count = [0]

            def seal(ins):
                ins.then_inc(step, 1)
                count[0] += 1
                dve.wait_ge(step, PER * n + count[0])
                dve.sem_inc(passed, 1)

            def top16(n_rows, values, spare, val, idx):
                for r in range(n_rows):
                    ins = nc.vector.max(val(r)[:, 0:8], values(r))
                seal(ins)
                for r in range(n_rows):
                    nc.vector.max_index(idx(r)[:, 0:8], val(r)[:, 0:8], values(r))
                dve.wait_ge(g_ready, HS + NB * GB * n)
                dve.sem_inc(passed, 1)
                for r in range(n_rows):
                    ins = nc.vector.match_replace(spare(r), val(r)[:, 0:8], values(r), NEG)
                seal(ins)
                for r in range(n_rows):
                    ins = nc.vector.max(val(r)[:, 8:16], spare(r))
                seal(ins)
                for r in range(n_rows):
                    ins = nc.vector.max_index(idx(r)[:, 8:16], val(r)[:, 8:16], spare(r))
                seal(ins)

            dve.wait_ge(s_copied, 4 * n + 4)
            if more:
                stage(n + 1)
            dve.sem_inc(passed, 1)
            top16(HP, lambda r: s[:, r], lambda r: s2[:, r], lambda r: top[:, r // 2, r % 2, :], lambda r: topi[:, r])
            seal(nc.vector.tensor_tensor(cand[:].rearrange("p h (a b) -> p h a b", a=TOPK),
                                         top[:, :, 0, :].unsqueeze(3).to_broadcast([P, RH, TOPK, TOPK]),
                                         top[:, :, 1, :].unsqueeze(2).to_broadcast([P, RH, TOPK, TOPK]), ALU.add))
            top16(RH, lambda r: cand[:, r], lambda r: cand2[:, r], lambda r: best[:, r], lambda r: besti[:, r])
            gate = rcg[:, 2].rearrange("p (h e) -> p h e", h=RH)
            nc.vector.tensor_tensor(gate, best[:], best[:, :, 0:1].to_broadcast([P, RH, TOPK]),
                                    ALU.subtract).then_inc(exp_in, 1)
            nc.vector.tensor_scalar(ab[:, 0], besti[:], 4, None, ALU.logical_shift_right)
            nc.vector.tensor_scalar(ab[:, 1], besti[:], TOPK - 1, None, ALU.bitwise_and)
            seal(nc.vector.tensor_copy(topf[:], topi[:].rearrange("p (h a) k -> p h a k", a=2)))
            seal(nc.vector.tensor_copy(abf[:], ab[:]))
            for half in range(2):
                seal(nc.vector.tensor_tensor(hot[:], abf[:, half].unsqueeze(3).to_broadcast([P, RH, TOPK, TOPK]), i16,
                                             ALU.is_equal))
                seal(nc.vector.tensor_tensor(hot[:], hot[:],
                                             topf[:, :, half].unsqueeze(2).to_broadcast([P, RH, TOPK, TOPK]),
                                             ALU.mult))
                nc.vector.tensor_reduce(rcg[:, half].rearrange("p (h e) -> p h e", h=RH), hot[:], AX.X,
                                        ALU.add).then_inc(rcg_ready, 1)
                dve.wait_ge(rcg_ready, 3 * n + half + 1)
            dve.wait_ge(exp_out, n + 1)
            seal(nc.vector.tensor_reduce(esum[:], gate, AX.X, ALU.add))
            seal(nc.vector.reciprocal(esum[:], esum[:]))
            assert count[0] == PER
            nc.vector.tensor_tensor(gate, gate, esum[:].unsqueeze(2).to_broadcast([P, RH, TOPK]),
                                    ALU.mult).then_inc(rcg_ready, 1)
            dve.wait_ge(rcg_copied, n + 1)
            dve.sem_inc(passed, 1)

            def one(b, u, k):
                for g in range(GB):
                    dve.wait_ge(g_ready, GB * b + g + 1)
                    tok = k * TB + GT * g
                    nc.vector.tensor_tensor(rows[:, g % HS], i128, spread(0, tok), ALU.is_equal)
                    if g % GE == 1:
                        ins = nc.vector.tensor_tensor(cols[:, g % HS], i128, spread(1, tok), ALU.is_equal)
                    else:
                        for t in range(GT):
                            ins = nc.vector.tensor_scalar(cols[:, g % HS, t], iota[:], rcgT[:, 1, bass.ds(tok + t, 1)],
                                                          rcgT[:, 2, bass.ds(tok + t, 1)], ALU.is_equal, ALU.mult)
                    ins.then_inc(hot_ready, 1)

            blocks(dve, n, one)

        tiles(dve, tile)

    @block.tensor
    def _(pe):
        pe.sem_inc(g_ready, HS)
        pe.wait_ge(k_in, 16)
        with pe.Fori(0, HP // 2) as i:
            for u in range(2):
                hp = 2 * i + u
                pe.wait_ge(wq_in[u], 16 * (i + 1))
                for half in range(2):
                    pe.wait_ge(km_copied, 2 * hp + half + 1)
                    for b in range(4):
                        c = 4 * half + b
                        ins = nc.tensor.matmul(s_ps[2 * u + half][:, b * NK:(b + 1) * NK], wq[:, u, c * P:(c + 1) * P],
                                               kT[:, hp, :], start=True, stop=True)
                    ins.then_inc(km_ready, 1)
        pe.wait_ge(km_copied, 4 + 2 * HP)

        def score(b):
            for c in range(DC):
                ins = nc.tensor.matmul(s_ps[b][:], ytile[:, c], km[:, c, b * HALF:(b + 1) * HALF], start=c == 0,
                                       stop=c == DC - 1)
            ins.then_inc(scored, 1)

        def u_unit(unit, col, half, chunks):
            if chunks[0] == 0:
                pe.wait_ge(unit_free, unit + 1)
                pe.wait_ge(u_split, col + 1)
            ins = split3(nc, u_ps[:], uc, yh, [(lambda t, c=c: t[:, c, :],
                                                lambda t, c=c: t[:, c, half * HALF:(half + 1) * HALF])
                                               for c in chunks], first=chunks[0] == 0, last=chunks[-1] == DC - 1)
            if chunks[-1] == DC - 1:
                ins.then_inc(unit_done, 1)

        pe.wait_ge(staged, 1)
        for b in range(4):
            score(b)

        def tile(n, more):
            if more:
                pe.wait_ge(s_copied, 4 * n + 4)
                pe.wait_ge(staged, n + 2)
            for k in range(4):
                if more and k in (0, 2):
                    for b in {0: (0,), 2: (1, 2)}[k]:
                        score(b)
                if k < 3:
                    u_unit(UU * n + k, UC * n + k // 2, k % 2, range(DC))
            if more:
                score(3)
            pe.wait_ge(rcg_ready, 3 * n + 3)
            for k in range(3):
                ins = nc.tensor.transpose(t_ps[:, k * P:(k + 1) * P], rcg[:, k], ident[:])
            ins.then_inc(rcg_turned, 1)
            u_unit(UU * n + 3, UC * n + 1, 1, range(DC))

            def one(b, u, k, i):
                for g in range(GB):
                    pe.wait_ge(hot_ready, GB * b + g + 1)
                    if g % GE == 1:
                        pe.wait_ge(cols_gated, GB // GE * b + g // GE + 1)
                    pe.wait_ge(g_copied, GB * b + g + 1)
                    for t in range(GT):
                        ins = nc.tensor.matmul(g_ps[g % 2][:, t * P:(t + 1) * P], rows[:, g % HS, t], cols[:, g % HS, t],
                                               start=True, stop=True)
                    ins.then_inc(g_ready, 1)
                    part = g - (0 if u else GB // 2)
                    if 0 <= part < GB // 2:
                        share = DC // (GB // 2)
                        u_unit(UU * n + 4 + 2 * i + u, UC * n + 2 + i, u, range(share * part, share * (part + 1)))

            blocks(pe, n, one, True)

        tiles(pe, tile)


JG = 2
NGRP = NK // JG
GP = UC * TT // JG


def build_experts(nc, ctx, uT, v, yh, g_scr, a_scr, acc):
    at = Place(nc)
    A = [[at(f"A{r}{s}", 0 + 16 * r + 8 * s, [P, JG, T], F32R) for s in range(2)] for r in range(2)]
    u_raw = at("u_raw", 128, [P, JG, DC, P])
    uw = [at(f"u{s}", 136 + 8 * s, [P, JG, DC, P], F32R) for s in range(2)]
    vw_even = [at(f"ve_even{s}", 136 + 8 * s, [P, JG, D], F32R) for s in range(2)]
    v_raw = at("v_raw", 152, [P, JG, D])
    vw = [at(f"ve{s}", 160 + 8 * s, [P, JG, D], F32R) for s in range(2)]
    g_sb = at("g_sb", 176, [P, 2, T // TB, JG, TB])
    act_sb = at("act_sb", 192, [P, JG, T])
    s_ps = [ctx.enter_context(nc.psum_tensor(f"e_s{i}", [P, HALF], F32)) for i in range(2 * JG)]
    o_ps = [ctx.enter_context(nc.psum_tensor(f"e_o{i}", [P, HALF], F32)) for i in range(4)]

    def sem(name):
        return ctx.enter_context(nc.semaphore("e_" + name))

    cleared, act_in = sem("cleared"), sem("act_in")
    u_in, u_free, u_hi, u_split, u_done = sem("u_in"), sem("u_free"), sem("u_hi"), sem("u_split"), sem("u_done")
    v_in, v_free, v_hi, v_split, v_done = sem("v_in"), sem("v_free"), sem("v_hi"), sem("v_split"), sem("v_done")
    g_in, g_free = [sem("g_in0"), sem("g_in1")], sem("g_free")
    gelu, gated, A_hi, A_split, added = sem("gelu"), sem("gated"), sem("A_hi"), sem("A_split"), sem("added")
    block = ctx.enter_context(nc.Block())
    NU, NV = 2 * JG, 2 * TT

    def groups(eng, first, pre, turn, both, last):
        first()
        with eng.Fori(0, GP // 2 - 1) as i:
            pre(2 * i, 0, i)
            pre(2 * i + 1, 1, i)
        pre(GP - 2, 0, GP // 2 - 1)
        turn(GP - 1, 1, GP // 2 - 1)
        with eng.Fori(GP // 2, NGRP // 2 - 1) as i:
            both(2 * i, 0, i)
            both(2 * i + 1, 1, i)
        both(NGRP - 2, 0, NGRP // 2 - 1)
        last(NGRP - 1, 1)

    def v_parts(g, r, pre):
        return vw_even if pre and r == 0 else vw

    @block.sync
    def _(sp):
        def load_u(g):
            sp.wait_ge(u_free, g - GP + 1)
            sp.dma_start(u_raw[:], uT[bass.ds(g * JG, JG)].rearrange("j p c i -> p j (c i)")).then_inc(u_in, 16)

        def load_v(g):
            sp.wait_ge(v_free, g + 1)
            sp.dma_start(v_raw[:], v[:, g]).then_inc(v_in, 16)

        def load_g(g, r):
            sp.wait_ge(g_free, g + 1)
            sp.dma_start(g_sb[:, r].rearrange("p b j t -> p b (j t)"),
                         g_scr[:, :, bass.ds(g * JG, JG), :].rearrange("p b j t -> p b (j t)")).then_inc(g_in[r], 16)

        def load_act(g):
            sp.wait_ge(A_split, JG * g + JG)
            sp.dma_start(act_sb[:], a_scr[:, bass.ds(g * JG, JG)]).then_inc(act_in, 16)

        def first():
            load_v(0)
            load_act(0)
            load_g(0, 0)
            load_v(1)
            load_g(1, 1)

        def pre(g, r, i):
            load_act(g + 1)
            load_v(g + 2)
            load_g(g + 2, r)

        def turn(g, r, i):
            sp.wait_ge(v_done, NV + NV * (g - 1) + NV)
            load_u(g + 1)
            load_g(g + 2, r)
            load_u(g + 2)

        def both(g, r, i):
            load_v(g + 1)
            if isinstance(g, int) and g == NGRP - 2:
                return
            load_g(g + 2, r)
            load_u(g + 2)

        groups(sp, first, pre, turn, both, lambda g, r: None)

    @block.scalar
    def _(act):
        def high_u(g):
            act.wait_ge(u_in, 16 * (g - GP + 1))
            act.wait_ge(u_done, NU * (g - GP) + NU)
            nc.scalar.activation(uw[0][:], u_raw[:], ACT.Copy).then_inc(u_hi, 1)

        def high_v(g, r, ahead=False):
            act.wait_ge(v_in, 16 * (g + 1))
            if ahead:
                act.wait_ge(v_done, NV * g)
            else:
                act.wait_ge(v_done, NV * g + NV)
            nc.scalar.activation(v_parts(g, r, ahead)[0][:], v_raw[:], ACT.Copy).then_inc(v_hi, 1)

        def activate(g, r):
            for j in range(JG):
                for half in range(2):
                    act.wait_ge(u_done, NU + NU * (g - GP) + 2 * j + half + 1)
                    act.wait_ge(A_split, JG * g + j + 1)
                    nc.scalar.activation(act_sb[:, j, half * HALF:(half + 1) * HALF], s_ps[2 * j + half][:],
                                         ACT.Gelu).then_inc(gelu, 1)
                if j:
                    high_a(g, r, j - 1)
            high_a(g, r, JG - 1)

        def high_a(g, r, j):
            act.wait_ge(gated, JG * g + j + 1)
            nc.scalar.activation(A[r][0][:, j], act_sb[:, j], ACT.Copy).then_inc(A_hi, 1)

        act.sem_inc(gelu, NU)

        def first():
            act.wait_ge(v_in, 16)
            nc.scalar.activation(vw_even[0][:], v_raw[:], ACT.Copy).then_inc(v_hi, 1)
            for j in range(JG):
                high_a(0, 0, j)

        def pre(g, r, i):
            if isinstance(g, int):
                high_v(g + 1, 1, True)
            else:
                high_v(g + 1, 1 - r, True)
            for j in range(JG):
                high_a(g + 1, 1 - r, j)

        def turn(g, r, i):
            high_u(g + 1)
            activate(g + 1, 1 - r)
            high_u(g + 2)

        def both(g, r, i):
            high_v(g, r)
            activate(g + 1, 1 - r)
            if not (isinstance(g, int) and g == NGRP - 2):
                high_u(g + 2)

        groups(act, first, pre, turn, both, high_v)

    @block.vector
    def _(dve):
        dve.sem_inc(u_free, 1)
        dve.sem_inc(v_free, 1)
        dve.sem_inc(g_free, 2)
        dve.sem_inc(A_split, JG)

        def low_u(g):
            dve.wait_ge(u_hi, g - GP + 1)
            nc.vector.tensor_tensor(uw[1][:], u_raw[:], uw[0][:].bitcast(F32), ALU.subtract).then_inc(u_split, 1)
            dve.wait_ge(u_split, g - GP + 1)
            dve.sem_inc(u_free, 1)

        def low_v(g, r, ahead=False):
            dve.wait_ge(v_hi, g + 1)
            part = v_parts(g, r, ahead)
            nc.vector.tensor_tensor(part[1][:], v_raw[:], part[0][:].bitcast(F32), ALU.subtract).then_inc(v_split, 1)
            dve.wait_ge(v_split, g + 1)
            dve.sem_inc(v_free, 1)

        def gate(g, r, k, between=nothing, loaded=False):
            dve.wait_ge(g_in[r], 16 * (k + 1))
            if loaded:
                dve.wait_ge(act_in, 16 * (g + 1))
            for j in range(JG):
                if not loaded:
                    dve.wait_ge(gelu, NU + NU * (g - GP) + 2 * j + 2)
                a = act_sb[:, j].rearrange("p (b t) -> p b t", t=TB)
                nc.vector.tensor_tensor(a, a, g_sb[:, r, :, j], ALU.mult).then_inc(gated, 1)
                if j:
                    low_a(g, r, j - 1)
            dve.wait_ge(gated, JG * g + JG)
            dve.sem_inc(g_free, 1)
            between(0, 2)
            low_a(g, r, JG - 1)

        def low_a(g, r, j):
            dve.wait_ge(A_hi, JG * g + j + 1)
            nc.vector.tensor_tensor(A[r][1][:, j], act_sb[:, j], A[r][0][:, j].bitcast(F32),
                                    ALU.subtract).then_inc(A_split, 1)

        def add(g, first=0, end=NV):
            for n in range(first, end):
                tt, half = n // 2, n % 2
                dve.wait_ge(v_done, NV + NV * g + n + 1)
                dve.wait_ge(added, NV * g + n + 1)
                sum_ = acc[:, tt, half * HALF:(half + 1) * HALF]
                nc.vector.tensor_tensor(sum_, sum_, o_ps[n % 4][:], ALU.add).then_inc(added, 1)

        def first():
            nc.vector.memset(acc[:], 0.0).then_inc(cleared, 1)
            dve.wait_ge(cleared, 1)
            dve.sem_inc(added, NV)
            low_v(0, 0, True)
            gate(0, 0, 0, loaded=True)

        def pre(g, r, i):
            low_v(g + 1, 1 - r, True)
            add(g, 0, 6)
            gate(g + 1, 1 - r, i + r, lambda first, end: add(g, 6, 8), True)
            add(g, 8)

        def turn(g, r, i):
            add(g, 0, 4)
            low_u(g + 1)
            add(g, 4)
            gate(g + 1, 1 - r, i + r)
            low_u(g + 2)

        def both(g, r, i):
            low_v(g, r)
            gate(g + 1, 1 - r, i + r, lambda first, end: add(g, first, end))
            add(g, 2, 4)
            if not (isinstance(g, int) and g == NGRP - 2):
                low_u(g + 2)
            add(g, 4)

        def last(g, r):
            low_v(g, r)
            add(g)

        groups(dve, first, pre, turn, both, last)

    @block.tensor
    def _(pe):
        def u_products(g):
            pe.wait_ge(u_split, g - GP + 1)
            for j in range(JG):
                for half in range(2):
                    pe.wait_ge(gelu, NU * (g - GP) + 2 * j + half + 1)
                    split3(nc, s_ps[2 * j + half][:], uw, yh,
                           [(lambda t, c=c: t[:, j, c, :], lambda t, c=c: t[:, c, half * HALF:(half + 1) * HALF])
                            for c in range(DC)]).then_inc(u_done, 1)

        def v_products(g, r, parts=vw):
            pe.wait_ge(v_split, g + 1)
            pe.wait_ge(A_split, JG + JG * g + JG)
            for n in range(NV):
                tt, half = n // 2, n % 2
                pe.wait_ge(added, NV + NV * g + n - 3)
                split3(nc, o_ps[n % 4][:], A[r], parts,
                       [(lambda t, j=j: t[:, j, tt * P:(tt + 1) * P],
                         lambda t, j=j: t[:, j, half * HALF:(half + 1) * HALF])
                        for j in range(JG)]).then_inc(v_done, 1)

        def first():
            pe.sem_inc(u_done, NU)
            pe.sem_inc(v_done, NV)

        def pre(g, r, i):
            v_products(g, r, v_parts(g, r, True))

        def turn(g, r, i):
            v_products(g, r)
            u_products(g + 1)

        def both(g, r, i):
            u_products(g + 1)
            v_products(g, r)

        groups(pe, first, pre, turn, both, v_products)


def build_second_norm(nc, ctx, passed, acc, y_scr, ln_g, ln_b, out):
    at = Place(nc)
    ys = at("ys", 96, [P, 2, D])
    z = at("z_e", 104, [P, D])
    yn = at("yn_e", 108, [P, 2, D])
    gb = at("gb_e", 116, [P, 2, D])
    st = at("st_e", 206.5, [P, 20])
    stats, mv, rstd, nmr, var, mhalf = (st[:, 0:12], st[:, 12:14], st[:, 14:15], st[:, 15:16], st[:, 16:17],
                                        st[:, 17:18])

    def sem(name):
        return ctx.enter_context(nc.semaphore("f_" + name))

    gb_in, const, y_in, z_ready, stat_step = sem("gb_in"), sem("const"), [sem("y_in0"), sem("y_in1")], sem(
        "z_ready"), sem("stat_step")
    rstd_ready, nmr_ready, yn_ready, scaled, ready, stored, freed = (
        sem("rstd_ready"), sem("nmr_ready"), sem("yn_ready"), sem("scaled"), sem("ready"), sem("stored"),
        sem("freed"))
    block = ctx.enter_context(nc.Block())

    def tiles(eng, body):
        with eng.Fori(0, TT // 2) as i:
            for u in range(2):
                body(2 * i + u, u, i)

    @block.sync
    def _(sp):
        sp.dma_start(gb[:, 0], ln_g.to_broadcast([P, D])).then_inc(gb_in, 16)
        sp.dma_start(gb[:, 1], ln_b.to_broadcast([P, D])).then_inc(gb_in, 16)

        def tile(n, u, i):
            sp.wait_ge(z_ready, n + 1)
            sp.dma_start(ys[:, u], y_scr[n]).then_inc(y_in[u], 16)

        tiles(sp, tile)

    @block.gpsimd
    def _(pool):
        nc.gpsimd.memset(mhalf, -0.5).then_inc(const, 1)
        pool.wait_ge(const, 1)

        def tile(n, u, i):
            pool.wait_ge(stat_step, 4 * n + 4)
            nc.gpsimd.tensor_tensor(rstd, var, mhalf, ALU.pow).then_inc(rstd_ready, 1)

        tiles(pool, tile)

    @block.scalar
    def _(act):
        act.sem_inc(yn_ready, 1)
        act.sem_inc(freed, 2)

        def tile(n, u, i):
            act.wait_ge(nmr_ready, n + 1)
            act.wait_ge(freed, n + 1)
            nc.scalar.activation(yn[:, u], z[:], ACT.Identity, scale=rstd, bias=nmr).then_inc(yn_ready, 1)
            act.wait_ge(ready, n + 1)
            act.dma_start(out[n], yn[:, u]).then_inc(stored, 16)
            act.wait_ge(stored, 16 * (n + 1))
            act.sem_inc(freed, 1)

        tiles(act, tile)

    @block.vector
    def _(dve):
        dve.sem_inc(z_ready, 2)
        dve.wait_ge(gb_in, 32)

        def tile(n, u, i):
            dve.wait_ge(y_in[u], 16 * (i + 1))
            dve.wait_ge(yn_ready, n + 1)
            nc.vector.scalar_tensor_tensor(z[:], ys[:, u], ALPHA, acc[:, n], ALU.mult, ALU.add).then_inc(z_ready, 1)
            dve.wait_ge(z_ready, n + 3)
            for half in range(2):
                nc.vector.bn_stats(stats[:, 6 * half:6 * half + 6],
                                   z[:, half * HALF:(half + 1) * HALF]).then_inc(stat_step, 1)
            dve.wait_ge(stat_step, 4 * n + 2)
            dve.sem_inc(passed, 1)
            nc.vector.bn_aggr(mv, stats).then_inc(stat_step, 1)
            dve.wait_ge(stat_step, 4 * n + 3)
            nc.vector.tensor_scalar(var, mv[:, 1:2], EPS, None, ALU.add).then_inc(stat_step, 1)
            dve.wait_ge(rstd_ready, n + 1)
            nc.vector.tensor_scalar(nmr, mv[:, 0:1], rstd, -1.0, ALU.mult, ALU.mult).then_inc(nmr_ready, 1)
            dve.wait_ge(yn_ready, n + 2)
            nc.vector.tensor_tensor(yn[:, u], yn[:, u], gb[:, 0], ALU.mult).then_inc(scaled, 1)
            dve.wait_ge(scaled, n + 1)
            nc.vector.tensor_tensor(yn[:, u], yn[:, u], gb[:, 1], ALU.add).then_inc(ready, 1)

        tiles(dve, tile)


def program(nc, a, out, debug):
    xT, w_in, subln = a["xT"], a["w_in"], a["subln"]
    lams = [a["lambda_" + n] for n in ("q1", "k1", "q2", "k2")]
    at = Place(nc)
    y_scr = nc.dram_tensor("y_scr", (TT, P, D), F32).ap()
    if debug not in ("A", "B"):
        g_scr = nc.dram_tensor("g_scr", (P, T // TB, NK, TB), F32).ap()
    xT_hi = at("xT_hi", 0, [P, DC, T], F32R)
    xT_lo = at("xT_lo", 32, [P, DC, T], F32R)
    oT = at("oT", 64, [P, H, T])
    ident = at("ident", 207.25, [P, P])
    passed = nc.alloc_semaphore("passed")
    with ExitStack() as ctx:
        build_attention(nc, ctx, passed, xT, w_in, lams, subln, (ident, None), None, xT_hi, xT_lo, oT)
    if debug != "A":
        merged = at("merged", 96, [P, DC, T])
        with ExitStack() as ctx:
            build_branches(nc, ctx, w_in, a["pool_w"], a["pool_scale"], a["b_gate"], a["w_branch"], (xT_hi, xT_lo), oT,
                           merged)
    if debug not in ("A", "B"):
        yT = at("yT", 64, [P, DC, T])
        with ExitStack() as ctx:
            build_first_norm(nc, ctx, passed, a["x"], a["w_out"], a["ln1_g"], a["ln1_b"], ident, merged, yT, y_scr)
        if debug != "C":
            yh = [at("yT_hi", 96, [P, DC, T], F32R), at("yT_lo", 64, [P, DC, T], F32R)]
            a_scr = nc.dram_tensor("a_scr", (P, UC * TT, T), F32).ap()
            with ExitStack() as ctx:
                build_retrieval(nc, ctx, passed, a["wqT"], a["keysT"], a["uT"], ident, yT, yh, g_scr, a_scr)
    if debug == "":
        acc = at("acc", 32, [P, TT, D])
        with ExitStack() as ctx:
            build_experts(nc, ctx, a["uT"], a["v"], yh, g_scr, a_scr, acc)
        with ExitStack() as ctx:
            build_second_norm(nc, ctx, passed, acc, y_scr, a["ln2_g"], a["ln2_b"], out[0].rearrange("(n p) d -> n p d", p=P))
    if debug in ("C", "G"):
        merged = yT
    if debug in ("A", "B", "C", "G"):
        oT = oT if debug == "A" else merged
        with ExitStack() as ctx:
            st = ctx.enter_context(nc.semaphore("st"))
            block = ctx.enter_context(nc.Block())

            @block.sync
            def _(sp):
                sp.dma_start(out[0].rearrange("(h p) t -> p h t", p=P), oT[:]).then_inc(st, 16)
                sp.wait_ge(st, 16)


def kernel(**inputs):
    import concourse.bacc as bacc
    from concourse.bass_utils import run_bass_kernel_spmd

    one = {name: np.asarray(a)[0] for name, a in inputs.items()}
    blocks = one["w_in"].reshape(DC, P, -1, P).transpose(2, 1, 0, 3)
    arrays = {"xT": one["x"].T, "w_in": blocks, "subln": one["subln_g"][:, None]}
    arrays["x"] = one["x"].reshape(TT, P, D) if one["x"].ndim == 2 else one["x"]
    for n in ("ln1_g", "ln1_b", "ln2_g", "ln2_b"):
        arrays[n] = one[n][None, :]
    arrays["w_out"] = one["w_out"]
    arrays["uT"] = one["peer_u"].reshape(NK, NK, DC, P).transpose(1, 3, 2, 0)
    arrays["v"] = one["peer_v"].reshape(NK, NGRP, JG, D)
    arrays["wqT"] = one["peer_wq"].T.reshape(2 * RH, P, D)
    arrays["keysT"] = one["peer_subkeys"].reshape(2 * RH, NK, P).transpose(2, 0, 1)
    arrays["pool_w"] = one["pool_w"].transpose(1, 0, 2)
    arrays["pool_scale"] = one["pool_scale"].reshape(PG, P).T
    arrays["b_gate"] = one["b_gate"].reshape(2 * DC, P).T
    arrays["w_branch"] = np.concatenate([one["w_attn_proj"], one["w_pool_proj"]]).reshape(
        CA + CP, P, DC, P).transpose(2, 1, 0, 3)
    for n in ("lambda_q1", "lambda_k1", "lambda_q2", "lambda_k2"):
        arrays[n] = one[n][None, :]
    arrays = {k: np.ascontiguousarray(v) for k, v in arrays.items()}
    nc = bacc.Bacc("TRN2", target_bir_lowering=False, num_devices=1)
    aps = {k: nc.dram_tensor(k, v.shape, F32, kind="ExternalInput").ap() for k, v in arrays.items()}
    out = nc.dram_tensor("out", (1, T, D), F32, kind="ExternalOutput").ap()
    program(nc, aps, out, DEBUG)
    return run_bass_kernel_spmd(nc, [arrays], core_ids=[0]).results[0]["out"]


DEBUG = ""
```
